# Optimizing a Trainium2 kernel written in Bass

```python
import math
import jax, jax.numpy as jnp
from jax import lax
import numpy as np

D_MODEL = 2048
BATCH = 1
SEQ = 256
DEPTH = 2

EXPAND = 2
W_MIX = EXPAND * D_MODEL
W_CONV = W_MIX // 2
CONV_GROUPS = 16
CONV_WIDTH = 3
N_RET_HEADS = 8
W_RET = W_MIX - W_CONV
RET_DV = W_RET // N_RET_HEADS
RET_DK = RET_DV // 2
W_QK = N_RET_HEADS * RET_DK
RET_CHUNK = 128
ROPE_THETA = 10000.0
NORM_EPS = 1e-6
W_IN_SPLITS = (W_CONV, W_CONV, W_CONV, W_CONV, W_QK, W_QK, W_RET, W_RET)
W_IN_TOTAL = sum(W_IN_SPLITS)

kernel_name = "hybrid_shortconv_retention_parallel_heads"

def _rmsnorm(x, gain):
    xf = x.astype(jnp.float32)
    y = xf * lax.rsqrt(jnp.mean(xf * xf, axis=-1, keepdims=True) + NORM_EPS)
    return (y * gain.astype(jnp.float32)).astype(x.dtype)

def _rope(t, positions):
    half = t.shape[-1] // 2
    inv_freq = ROPE_THETA ** (-jnp.arange(half, dtype=jnp.float32) / half)
    ang = positions.astype(jnp.float32)[..., None] * inv_freq
    cos, sin = jnp.cos(ang)[:, :, None, :], jnp.sin(ang)[:, :, None, :]
    tf = t.astype(jnp.float32)
    t1, t2 = tf[..., :half], tf[..., half:]
    return jnp.concatenate([t1 * cos - t2 * sin, t1 * sin + t2 * cos], axis=-1)

def _causal_short_conv(u, w):
    s = u.shape[1]
    up = jnp.pad(u, ((0, 0), (CONV_WIDTH - 1, 0), (0, 0)))
    return sum(w[k] * up[:, k:k + s] for k in range(CONV_WIDTH))

def _retention_chunkwise(q, k, v):
    b, s, h, dk = q.shape
    dv = v.shape[-1]
    n = s // RET_CHUNK
    log_gamma = jnp.log(1.0 - 2.0 ** (-5.0 - jnp.arange(h, dtype=jnp.float32)))
    idx = jnp.arange(RET_CHUNK, dtype=jnp.float32)
    diff = idx[:, None] - idx[None, :]
    decay_in = jnp.where(diff[None] >= 0,
                         jnp.exp(jnp.maximum(diff, 0.0)[None] * log_gamma[:, None, None]), 0.0)
    zeta = jnp.exp((RET_CHUNK - 1 - idx)[:, None] * log_gamma[None])
    xi = jnp.exp((idx + 1.0)[:, None] * log_gamma[None])
    gamma_chunk = jnp.exp(RET_CHUNK * log_gamma)

    qc = q.reshape(b, n, RET_CHUNK, h, dk)
    kc = k.reshape(b, n, RET_CHUNK, h, dk)
    vc = v.reshape(b, n, RET_CHUNK, h, dv)

    scores = jnp.einsum('bnihd,bnjhd->bnhij', qc, kc) * decay_in[None, None]
    inner = jnp.einsum('bnhij,bnjhe->bnihe', scores, vc)

    kv = jnp.einsum('bnjhd,bnjhe->bnhde', kc * zeta[None, None, :, :, None], vc)

    def step(state, kv_i):
        return gamma_chunk[None, :, None, None] * state + kv_i, state

    _, states_prev = lax.scan(step, jnp.zeros((b, h, dk, dv), jnp.float32), jnp.moveaxis(kv, 1, 0))
    states_prev = jnp.moveaxis(states_prev, 0, 1)
    cross = jnp.einsum('bnihd,bnhde->bnihe', qc, states_prev) * xi[None, None, :, :, None]
    return (inner + cross).reshape(b, s, h, dv)

def _head_groupnorm(y, gain):
    mu = jnp.mean(y, axis=-1, keepdims=True)
    var = jnp.mean(jnp.square(y - mu), axis=-1, keepdims=True)
    yn = (y - mu) * lax.rsqrt(var + NORM_EPS)
    return yn.reshape(y.shape[0], y.shape[1], -1) * gain.astype(jnp.float32)

def _mixer_layer(x, c, positions, norm_pre, norm_post, w_ada, b_ada, w_in, conv_w, gn_gain, w_out):
    b, s, _ = x.shape
    mod = jax.nn.silu(c) @ w_ada + b_ada
    shift, scale, gate = jnp.split(mod, 3, axis=-1)
    h = _rmsnorm(x, norm_pre) * (1.0 + scale[:, None, :]) + shift[:, None, :]

    z = h @ w_in
    offs = list(np.cumsum(W_IN_SPLITS)[:-1])
    gb, gcin, u, g_c, q, k, v, g_r = jnp.split(z, offs, axis=-1)

    y_conv = gb * _causal_short_conv(gcin * u, conv_w)
    y_conv = y_conv * jax.nn.silu(g_c)

    q = _rope(q.reshape(b, s, N_RET_HEADS, RET_DK), positions)
    k = _rope(k.reshape(b, s, N_RET_HEADS, RET_DK), positions) * (RET_DK ** -0.5)
    v = v.reshape(b, s, N_RET_HEADS, RET_DV).astype(jnp.float32)
    ret = _head_groupnorm(_retention_chunkwise(q, k, v), gn_gain).astype(x.dtype)
    y_ret = ret * jax.nn.silu(g_r)

    o = jnp.concatenate([y_conv, y_ret], axis=-1) @ w_out
    return x + gate[:, None, :] * _rmsnorm(o, norm_post)

def setup_inputs(seed: int = 0) -> dict:
    key = jax.random.key(seed)
    ks = jax.random.split(key, 12)
    f32 = jnp.float32
    x = jax.random.normal(ks[0], (BATCH, SEQ, D_MODEL), f32)
    c = jax.random.normal(ks[1], (BATCH, D_MODEL), f32)
    offset = jax.random.randint(ks[2], (BATCH, 1), 0, 1024, dtype=jnp.int32)
    positions = jnp.arange(SEQ, dtype=jnp.int32)[None, :] + offset
    norm_pre = 1.0 + 0.05 * jax.random.normal(ks[3], (DEPTH, D_MODEL), f32)
    norm_post = 1.0 + 0.05 * jax.random.normal(ks[4], (DEPTH, D_MODEL), f32)
    w_ada = 0.1 * D_MODEL ** -0.5 * jax.random.normal(ks[5], (DEPTH, D_MODEL, 3 * D_MODEL), f32)
    b_ada = 0.01 * jax.random.normal(ks[6], (DEPTH, 3 * D_MODEL), f32)
    w_in = D_MODEL ** -0.5 * jax.random.normal(ks[7], (DEPTH, D_MODEL, W_IN_TOTAL), f32)
    conv_w = CONV_WIDTH ** -0.5 * jax.random.normal(ks[8], (DEPTH, CONV_WIDTH, W_CONV), f32)
    gn_gain = 1.0 + 0.05 * jax.random.normal(ks[9], (DEPTH, W_RET), f32)
    w_out = W_MIX ** -0.5 * jax.random.normal(ks[10], (DEPTH, W_MIX, D_MODEL), f32)
    return {"x": x, "c": c, "positions": positions, "norm_pre": norm_pre, "norm_post": norm_post,
            "w_ada": w_ada, "b_ada": b_ada, "w_in": w_in, "conv_w": conv_w,
            "gn_gain": gn_gain, "w_out": w_out}

def reference(x, c, positions, norm_pre, norm_post, w_ada, b_ada, w_in, conv_w, gn_gain, w_out):
    for l in range(DEPTH):
        x = _mixer_layer(x, c, positions, norm_pre[l], norm_post[l], w_ada[l], b_ada[l],
                         w_in[l], conv_w[l], gn_gain[l], w_out[l])
    return x


_drawn_inputs = setup_inputs


def setup_inputs(seed=0):
    import zlib

    import numpy as np

    out = dict(_drawn_inputs(seed))
    spreads = {}
    factors = {'norm_pre': 6.423, 'norm_post': 8.0, 'b_ada': 3.971, 'gn_gain': 200.0}
    for name, (base, spread) in spreads.items():
        noise = np.random.default_rng([zlib.crc32(name.encode()), seed]).standard_normal(out[name].shape)
        drawn = base * np.exp(spread * noise) if base else spread * noise
        out[name] = __import__('jax').numpy.asarray(drawn.astype(out[name].dtype))
    for name, factor in factors.items():
        out[name] = (out[name] * factor).astype(out[name].dtype)
    return out
```

```python
import math
from contextlib import ExitStack

import numpy as np

import concourse.bass as bass
from concourse import mybir

F32 = mybir.dt.float32
F32R = mybir.dt.float32r
I32 = mybir.dt.int32
ALU = mybir.AluOpType
ACT = mybir.ActivationFunctionType

P = 128
D = 2048
S = 256
LAYERS = 2
KT = D // P
NT = S // P
W_CONV = 2048
HEADS = 8
DK, DV = 128, 256
W_QK = HEADS * DK
CONV_K = 3
EPS = 1e-6
COL_GB, COL_GC, COL_U, COL_G = 0, W_CONV, 2 * W_CONV, 3 * W_CONV
COL_Q = 4 * W_CONV
COL_V = COL_Q + 2 * W_QK
COL_GR = COL_V + HEADS * DV
BLK = 512
TILES = BLK // P
CK = 4
GROUPS = KT // CK
SLOTS = 4
QK, VV, GR, GC, UU, GB, GG = range(7)
BLOCKS = 7
TURNS = 4
CH_TURN = BLOCKS * GROUPS
CH_OUT = (2 * D // (CK * P)) * (D // BLK)
OUT_CH = 2 * D // (CK * P)
CH_LAYER = TURNS * CH_TURN + CH_OUT
ADA_START = 8
ADA_TURN = (3, 1)
Z_TURN = 26
Z_OUT = D // P
Z_LAYER = TURNS * Z_TURN + Z_OUT
LO_TURN = 24
LO_LAYER = TURNS * LO_TURN + Z_OUT
PRM_B, PRM_PRE, PRM_POST, PRM_GN, PRM_C, PRM_CW = 0, 96, 128, 160, 192, 208
PRM = 304


def ada_before(layer):
    n = ADA_TURN[layer] * GROUPS
    at = [0] * (CH_TURN + 1)
    for i in range(n):
        at[1 + (i * (CH_TURN - 1)) // n] += 1
    return at


def mod_points(layer):
    return (VV, UU, GG) if layer == 0 else (GG,)


def build(nc, x, c, positions, norm_pre, norm_post, w_ada, b_ada, w_in, conv_w, gn_gain, w_out,
          consts, decay, out):
    ctx = ExitStack()
    with ctx:
        def sb(name, shape, dt=F32):
            return ctx.enter_context(nc.sbuf_tensor(name, shape, dt))

        def sem(name):
            return ctx.enter_context(nc.semaphore(name))

        xT = sb("xT", [P, KT, S])
        H = sb("H", [P, KT, 2 * S], F32R)
        Y2 = sb("Y2", [P, KT, 2 * S], F32R)
        yr = sb("yr", [P, KT, S])
        stage = sb("stage", [P, SLOTS, CK, BLK])
        w_hi = sb("w_hi", [P, 4, 2, BLK], F32R)
        w_lo = sb("w_lo", [P, 4, 2, BLK], F32R)
        bufA = sb("bufA", [P, 4, S])
        bufB = sb("bufB", [P, 4, S])
        bufC = sb("bufC", [P, 4, S])
        cu = sb("cu", [P, 4, S + 2])
        v_sb = sb("v_sb", [P, NT, 2 * DV])
        sg = sb("sg", [P, 4, S])
        p_sb = sb("p_sb", [P, 2, 3 * P])
        lo_sb = sb("lo_sb", [P, 2, S])
        dec = sb("dec", [P, 2, S])
        cos_t = sb("cos_t", [P, S])
        sin_t = sb("sin_t", [P, S])
        acc = sb("acc", [P, BLK])
        acc_hi = sb("acc_hi", [P, BLK], F32R)
        acc_lo = sb("acc_lo", [P, BLK], F32R)
        ident = sb("ident", [P, P + 2])
        ones = sb("ones", [P, P])
        ones_r = sb("ones_r", [P, 2], F32R)
        prm = sb("prm", [P, PRM])
        mod = sb("mod", [P, LAYERS * 3 * KT])
        c_silu = sb("c_silu", [P, KT])
        ga = sb("ga", [P, KT])
        gp = sb("gp", [P, KT])
        stats = sb("stats", [P, 4, 6])
        mv = sb("mv", [P, 4, 2])
        rs4 = sb("rs4", [P, 4])
        mhalf = sb("mhalf", [P, 4])
        var_t = lo_sb[:, 0, :]
        rt = lo_sb[:, 1, :]
        tmp_t = sb("tmp_t", [P, S])

        Z = [ctx.enter_context(nc.psum_tensor(f"Z{t}", [P, 2 * S], F32)) for t in range(4)]
        SC = [ctx.enter_context(nc.psum_tensor(f"SC{t}", [P, 2 * S], F32)) for t in range(2)]
        IN = [ctx.enter_context(nc.psum_tensor(f"IN{t}", [P, 2 * S], F32)) for t in range(2)]

        s_par = sem("params_loaded")
        s_x = sem("x_loaded")
        s_pos = sem("positions_loaded")
        s_dec = sem("decay_loaded")
        s_stage = [sem(f"stage_loaded{i}") for i in range(SLOTS)]
        s_k = [sem(f"k_columns_loaded{i}") for i in range(GROUPS)]
        s_used = sem("stage_used")
        s_hi = sem("hi_done")
        s_lo = sem("lo_done")
        s_pe = sem("pe_tiles")
        s_zlo = sem("z_lo_copied")
        s_z = sem("z_free")
        s_swap = sem("qk_swapped")
        s_rope = sem("rope_done")
        s_sgr = sem("silu_gr_done")
        s_sc = sem("scores_done")
        s_p = sem("p_done")
        s_in = sem("inner_done")
        s_mv = sem("head_stats_done")
        s_rs = sem("head_rstd_done")
        s_yn = sem("heads_normalised")
        s_tr = sem("heads_transposed")
        s_yr = sem("yret_done")
        s_cu = sem("cu_done")
        s_cv = sem("conv_done")
        s_cg = sem("conv_gated")
        s_sg = sem("silu_g_done")
        s_y = sem("yconv_done")
        s_yhi = sem("y_hi_done")
        s_y2 = sem("yconv_split")
        s_hr = sem("yret_split")
        s_acc = sem("ada_acc_done")
        s_ahi = sem("ada_hi_done")
        s_alo = sem("ada_lo_done")
        s_mm = sem("ada_summed")
        s_mod = sem("mod_done")
        s_o = sem("o_squared")
        s_osum = sem("o_summed")
        s_xn = sem("x_new")
        s_xsq = sem("x_squared")
        s_xsum = sem("x_summed")
        s_var = sem("variance_done")
        s_sqrt = sem("sqrt_done")
        s_hf = sem("h_done")
        s_h = sem("h_split")
        s_tp = sem("start_transposes")
        s_tpc = sem("start_copied")
        s_cs = sem("c_silu_done")
        s_tab = sem("angle_done")
        s_sin = sem("sines_done")
        s_rot = sem("tables_done")
        s_ot = sem("out_transposed")
        s_oc = [sem("out_copied_v"), sem("out_copied_s")]
        s_out = sem("out_stored")
        s_vd = sem("vector_step")
        s_pd = sem("pool_step")
        s_ad = sem("scalar_step")

        s_held = {e: sem(f"{e}_held") for e in ("sp", "dve", "pool")}

        block = ctx.enter_context(nc.Block())

        def hold(eng, name):
            eng.sem_inc(s_held[name], 1)

        class Steps:

            def __init__(self, eng, s):
                self.eng, self.s, self.n, self.turn, self.per = eng, s, 0, None, 0

            def then(self, ins):
                ins.then_inc(self.s, 1)
                self.n += 1
                self.last = self.n if self.turn is None else self.n + self.turn * self.per

            def wait(self):
                self.eng.wait_ge(self.s, self.last)

            def loop(self, turn, per):
                self.turn, self.per, self.at = turn, per, self.n

            def end(self, turns):
                assert self.n - self.at == self.per, (self.n - self.at, self.per)
                self.n += self.per * (turns - 1)
                self.turn = None

        def stage_pos(layer, j, w):
            base = ADA_START * GROUPS
            for earlier in range(layer):
                base += TURNS * (CH_TURN + ADA_TURN[earlier] * GROUPS) + CH_OUT
            return base + w + sum(ada_before(layer)[:w + 1]) + j * (CH_TURN + ADA_TURN[layer] * GROUPS)

        def out_pos(layer, nb, w):
            return stage_pos(layer, TURNS, 0) + OUT_CH * nb + w

        def ck(layer, j, w):
            return CH_LAYER * layer + w + j * CH_TURN

        def ck_out(layer, nb, w):
            return CH_LAYER * layer + TURNS * CH_TURN + w + nb * OUT_CH

        def z_at(layer, j, b):
            return 4 + Z_LAYER * layer + 4 * b - (2 if b > VV else 0) + j * Z_TURN

        def zlo_at(layer, j, b):
            return LO_LAYER * layer + 4 * b - (4 if b > VV else 0) + j * LO_TURN

        def z_out(layer, nb):
            return 4 + Z_LAYER * layer + TURNS * Z_TURN + nb * 4

        def zlo_out(layer, nb):
            return LO_LAYER * layer + TURNS * LO_TURN + nb * 4

        def ada_no(layer, j, m):
            return ADA_START + (TURNS * ADA_TURN[0] if layer else 0) + m + j * ADA_TURN[layer]

        ADA_WHAT = (((0, 2), (1, 1), (1, 0)), ((1, 2),))

        @block.sync
        def _(sp):
            def load(slot, pos, dst, src, first=False):
                if not first:
                    sp.wait_ge(s_used, pos - SLOTS + 1)
                    hold(sp, "sp")
                sp.dma_start(dst, src).then_inc(s_stage[slot], 16)

            def rows(w, kc):
                return w[kc * CK * P:(kc + 1) * CK * P, :].rearrange("(a p) n -> p a n", p=P)

            sp.dma_start(ident[:, :], consts).then_inc(s_par, 16)
            pr = yr[:, :, :].rearrange("p t s -> p (t s)")
            for l in range(LAYERS):
                sp.dma_start(bufA[48 * l:48 * l + 48, 0, 0:P],
                             b_ada[l, :].rearrange("(r q) -> r q", q=P)).then_inc(s_par, 16)
                for i, g in enumerate((norm_pre, norm_post, gn_gain)):
                    r = 32 * i + 16 * l
                    sp.dma_start(bufA[r:r + 16, 1, 0:P],
                                 g[l, :].rearrange("(r q) -> r q", q=P)).then_inc(s_par, 16)
                sp.dma_start(bufA[48 * l:48 * l + 48, 2, 0:P],
                             conv_w[l, :, :].rearrange("k (r q) -> (k r) q", q=P)).then_inc(s_par, 16)
            sp.dma_start(bufA[96:112, 1, 0:P], c[0, :].rearrange("(r q) -> r q", q=P)).then_inc(s_par, 16)
            for i in range(NT):
                sp.dma_start(pr[:, i * D:(i + 1) * D], x[0, i * P:(i + 1) * P, :]).then_inc(s_x, 16)
            sp.dma_start(dec[:, :, :], decay[0, :, :, :]).then_inc(s_dec, 16)
            pos = 0
            for g in range(GROUPS):
                for part in (1, 0):
                    for kc in range(GROUPS):
                        col = part * D + g * BLK
                        load(pos % SLOTS, pos, stage[:, pos % SLOTS, :, :],
                             rows(w_ada[0, :, :], kc)[:, :, col:col + BLK], first=pos < SLOTS)
                        pos += 1
            for l in range(LAYERS):
                before = ada_before(l)
                with sp.Fori(0, TURNS) as j:
                    slot0 = stage_pos(l, 0, 0) % SLOTS
                    assert slot0 == 0
                    ada = 0
                    for w in range(CH_TURN + 1):
                        for i in range(before[w]):
                            al, part = ADA_WHAT[l][ada // GROUPS]
                            rel = stage_pos(l, 0, w) - before[w] + i
                            p = stage_pos(l, j, w) - before[w] + i
                            load(rel % SLOTS, p, stage[:, rel % SLOTS, :, :],
                                 rows(w_ada[al, :, :], ada % GROUPS)[:, :, bass.ds(j * BLK + part * D, BLK)])
                            ada += 1
                        if w == CH_TURN:
                            break
                        rel, p = stage_pos(l, 0, w), stage_pos(l, j, w)
                        b, kc = divmod(w, GROUPS)
                        dst = stage[:, rel % SLOTS, :, :]
                        src = rows(w_in[l, :, :], kc)
                        if b == QK:
                            sp.wait_ge(s_used, p - SLOTS + 1)
                            hold(sp, "sp")
                            sp.dma_start(dst[:, :, 0:2 * DK], src[:, :, bass.ds(j * 2 * DK + COL_Q, 2 * DK)])\
                                .then_inc(s_stage[rel % SLOTS], 16)
                            sp.dma_start(dst[:, :, 2 * DK:], src[:, :, bass.ds(j * 2 * DK + COL_Q + W_QK, 2 * DK)])\
                                .then_inc(s_k[kc], 16)
                        else:
                            col = {VV: COL_V, GR: COL_GR, GC: COL_GC, UU: COL_U, GB: COL_GB, GG: COL_G}[b]
                            load(rel % SLOTS, p, dst, src[:, :, bass.ds(j * BLK + col, BLK)])
                        if w == CH_TURN - 4:
                            sp.wait_ge(s_p, 2 * TURNS * l + 2 + 2 * j)
                            hold(sp, "sp")
                            sp.dma_start(dec[:, :, :], decay[bass.ds(j + 1, 1), :, :, :]
                                         .rearrange("o p h s -> p (o h) s")).then_inc(s_dec, 16)
                sp.sem_inc(s_k[0], 16)
                with sp.Fori(0, D // BLK) as nb:
                    for w in range(OUT_CH):
                        load(w % SLOTS, out_pos(l, nb, w), stage[:, w % SLOTS, :, :],
                             rows(w_out[l, :, :], w)[:, :, bass.ds(nb * BLK, BLK)])
            for g in range(GROUPS):
                for i in range(NT):
                    sp.wait_ge(s_oc[i], g + 1)
                    sp.dma_start(out[0, i * P:(i + 1) * P, g * BLK:(g + 1) * BLK],
                                 stage[:, i, g, :]).then_inc(s_out, 16)
            sp.wait_ge(s_out, 16 * GROUPS * NT)

        @block.scalar
        def _(act):
            def split(slot, value, parity, n):
                act.wait_ge(s_stage[slot], value)
                act.wait_ge(s_pe, 4 * n + 4)
                for h in range(2):
                    nc.scalar.copy(w_hi[:, 2 * parity + h, :, :],
                                   stage[:, slot, 2 * h:2 * h + 2, :]).then_inc(s_hi, 1)

            def z_low(pe, t, zlo, z):
                act.wait_ge(s_pe, pe)
                act.wait_ge(s_z, z)
                nc.scalar.copy(lo_sb[:, t % 2, :], Z[t][:, S:2 * S]).then_inc(s_zlo, 1)

            def ada_hi(k):
                act.wait_ge(s_acc, k + 1)
                act.wait_ge(s_mm, k)
                nc.scalar.copy(acc_hi[:, :], acc[:, :]).then_inc(s_ahi, 1)

            def sqrt(k):
                act.wait_ge(s_var, k)
                nc.scalar.activation(rt, var_t, ACT.Sqrt).then_inc(s_sqrt, 1)

            def x_squares(base, k):
                for g in range(GROUPS):
                    act.wait_ge(s_xn, base + g + 1)
                    if g >= 2:
                        act.wait_ge(s_xsum, KT * k + 4 * (g - 1))
                    nc.scalar.activation((bufA, bufB)[g % 2][:, :, :], xT[:, 4 * g:4 * g + 4, :],
                                         ACT.Square).then_inc(s_xsq, 1)

            def h_hi(g, n, yhi):
                act.wait_ge(s_hf, n)
                nc.scalar.copy(H[:, 4 * g:4 * g + 4, 0:S], (bufA, bufB)[g % 2][:, :, :]).then_inc(s_yhi, 1)

            act.dma_start(bufC[:, 0, :].bitcast(I32), 
                          positions.rearrange("a s -> (a s)").partition_broadcast(P)).then_inc(s_pos, 16)
            act.wait_ge(s_tpc, 3)
            nc.scalar.activation(c_silu[:, :], prm[:, PRM_C:PRM_C + KT], ACT.Silu).then_inc(s_cs, 1)
            x_squares(0, 0)
            sqrt(1)
            act.wait_ge(s_tab, 1)
            nc.scalar.activation(sin_t[:, :], bufC[:, 1, :], ACT.Sin).then_inc(s_sin, 1)
            nc.scalar.activation(cos_t[:, :], bufC[:, 1, :], ACT.Sin, scale=0.5).then_inc(s_sin, 1)
            for g in range(GROUPS):
                ada_hi(2 * g)
                ada_hi(2 * g + 1)
                h_hi(g, g + 1, g + 1)

            for l in range(LAYERS):
                before = ada_before(l)
                span = CH_TURN + ADA_TURN[l] * GROUPS
                if l == 0:
                    p0 = stage_pos(l, 0, 0)
                    act.wait_ge(s_k[0], 16)
                    split(p0 % SLOTS, 16 * (p0 // SLOTS + 1), 0, 0)
                else:
                    for g in range(GROUPS):
                        h_hi(g, GROUPS + g + 1, 0)
                with act.Fori(0, TURNS) as j:
                    seen = 0
                    for w in range(1, CH_TURN + 1):
                        for _ in range(before[w]):
                            seen += 1
                            if seen % GROUPS == 0:
                                ada_hi(ada_no(l, j, seen // GROUPS - 1))
                        rel = stage_pos(l, 0, w)
                        if w < GROUPS:
                            act.wait_ge(s_k[w], j * 16 + 16 * (TURNS * l + 1))
                        if w == CH_TURN:
                            act.wait_ge(s_k[0], j * 16 + 16 * ((TURNS + 1) * l + 2))
                        split(rel % SLOTS, j * (16 * span // SLOTS) + 16 * (rel // SLOTS + 1), w % 2, ck(l, j, w))
                        if w % GROUPS:
                            continue
                        b = w // GROUPS - 1
                        if b != VV:
                            for t in range(TILES):
                                z_low(8 + 4 * ck(l, j, w - 1) + t + 1, t, zlo_at(l, j, b), z_at(l, j, b) + max(0, t - 1))
                        if b == QK:
                            act.wait_ge(s_z, z_at(l, j, b + 1))
                            nc.scalar.copy(bufB[64:128, :, :], bufA[0:64, :, :]).then_inc(s_swap, 1)
                            nc.scalar.copy(bufB[0:64, :, :], bufA[64:128, :, :]).then_inc(s_swap, 1)
                        if b == GR:
                            act.wait_ge(s_z, z_at(l, j, b + 1))
                            nc.scalar.activation(sg[:, :, :], sg[:, :, :], ACT.Silu).then_inc(s_sgr, 1)
                        if b == GG:
                            act.wait_ge(s_z, z_at(l, j, b + 1))
                            nc.scalar.activation(bufA[:, :, :], bufA[:, :, :], ACT.Silu).then_inc(s_sg, 1)
                            act.wait_ge(s_y, TURNS * l + 1 + j)
                            nc.scalar.copy(Y2[:, bass.ds(j * 4, 4), 0:S], bufC[:, :, :]).then_inc(s_yhi, 1)

                def out_block(nb, first=False, last=False):
                    for w in range(1, OUT_CH + (0 if last else 1)):
                        pos = out_pos(l, 0, w)
                        if isinstance(nb, int) and nb == 3 and w == OUT_CH:
                            act.wait_ge(s_k[0], 16 * ((TURNS + 1) * (l + 1) + 1))
                        split(w % SLOTS, nb * (16 * OUT_CH // SLOTS) + 16 * (pos // SLOTS + 1), w % 2,
                              ck_out(l, nb, w))
                        if first and w <= GROUPS:
                            if w == 1:
                                act.wait_ge(s_pe, 8 + 4 * ck_out(l, 0, 0))
                                act.wait_ge(s_yr, 4 + 4 * TURNS * (l + 1))
                            nc.scalar.copy(H[:, 4 * w - 4:4 * w, 0:S], yr[:, 4 * w - 4:4 * w, :]).then_inc(s_yhi, 1)
                    for t in range(TILES):
                        z_low(8 + 4 * ck_out(l, nb, OUT_CH - 1) + t + 1, t, 0, z_out(l, nb) + max(0, t - 1))
                    if not first or l:
                        act.wait_ge(s_osum, KT * l + 4 * nb)
                    for t in range(TILES):
                        act.wait_ge(s_z, z_out(l, nb) + t + 1)
                        nc.scalar.activation(bufA[:, t, :], yr[:, bass.ds(nb * 4 + t, 1), :].rearrange("p o s -> p (o s)")
                                             if not isinstance(nb, int) else yr[:, nb * 4 + t, :],
                                             ACT.Square).then_inc(s_o, 1)

                out_block(0, first=True)
                with act.Fori(1, 3) as nb:
                    out_block(nb)
                out_block(3, last=l == LAYERS - 1)
                sqrt(2 * l + 2)
                if l < LAYERS - 1:
                    x_squares(GROUPS * (l + 1), l + 1)
                    sqrt(2 * l + 3)
            for g in range(GROUPS):
                act.wait_ge(s_ot, 2 * g + 2)
                nc.scalar.copy(stage[:, 1, g, :], (SC, IN)[g % 2][1][:, :]).then_inc(s_oc[1], 1)

        @block.vector
        def _(dve):
            me = Steps(dve, s_vd)
            V = nc.vector

            def split(slot, value, parity, n):
                for h in range(2):
                    dve.wait_ge(s_hi, 2 * n + h + 1)
                    ins = V.tensor_tensor(w_lo[:, 2 * parity + h, :, :], stage[:, slot, 2 * h:2 * h + 2, :],
                                          w_hi[:, 2 * parity + h, :, :].bitcast(F32), ALU.subtract)
                    ins.then_inc(s_lo, 1)
                dve.wait_ge(s_lo, 2 * n + 2)

            def ada_chunk(slot, value, kc):
                dve.wait_ge(s_stage[slot], value)
                for a in range(CK):
                    k = CK * kc + a
                    w = stage[:, slot, a, :]
                    if k == 0:
                        ins = V.tensor_scalar(acc[:, :], w, c_silu[:, 0:1], None, ALU.mult)
                    else:
                        me.wait()
                        ins = V.scalar_tensor_tensor(acc[:, :], w, c_silu[:, k:k + 1], acc[:, :],
                                                     ALU.mult, ALU.add)
                    me.then(ins)
                me.wait()
                used()

            def ada_low(k):
                dve.wait_ge(s_ahi, k + 1)
                V.tensor_tensor(acc_lo[:, :], acc[:, :], acc_hi[:, :].bitcast(F32), ALU.subtract).then_inc(s_alo, 1)

            def used():
                dve.sem_inc(s_used, 1)

            def mods(k, col):
                dve.wait_ge(s_mm, k + 1)
                V.tensor_tensor(mod[:, bass.ds(col, 4)], IN[1][:, 0:8:2], prm[:, bass.ds(col, 4)], ALU.add)\
                    .then_inc(s_mod, 1)

            def z_out_of(t, zlo, dst):
                dve.wait_ge(s_zlo, zlo)
                V.tensor_tensor(dst, Z[t][:, 0:S], lo_sb[:, t % 2, :], ALU.add).then_inc(s_z, 1)

            def rstd(k, sources):
                for i, src in enumerate(sources):
                    if i == 0:
                        ins = V.tensor_scalar(var_t, src, 1.0 / D, EPS, ALU.mult, ALU.add)
                    else:
                        me.wait()
                        ins = V.scalar_tensor_tensor(var_t, src, 1.0 / D, var_t, ALU.mult, ALU.add)
                    me.then(ins)
                me.wait()
                dve.sem_inc(s_var, 1)
                dve.wait_ge(s_sqrt, k)
                me.then(V.reciprocal(rt, rt))
                me.wait()
                me.then(V.tensor_tensor(tmp_t[:, :], rt, rt, ALU.mult))
                me.wait()
                me.then(V.tensor_tensor(tmp_t[:, :], tmp_t[:, :], var_t, ALU.mult))
                me.wait()
                me.then(V.tensor_scalar(tmp_t[:, :], tmp_t[:, :], -0.5, 1.5, ALU.mult, ALU.add))
                me.wait()
                me.then(V.tensor_tensor(rt, rt, tmp_t[:, :], ALU.mult))
                me.wait()

            def rt4():
                return rt.rearrange("p (o s) -> p o s", o=1).broadcast_to([P, 4, S])

            def h_group(l, g, n):
                buf = (bufA, bufB)[g % 2]
                me.then(V.scalar_tensor_tensor(ga[:, 4 * g:4 * g + 4], mod[:, 48 * l + KT + 4 * g:48 * l + KT + 4 * g + 4],
                                               1.0, prm[:, PRM_PRE + KT * l + 4 * g:PRM_PRE + KT * l + 4 * g + 4],
                                               ALU.add, ALU.mult))
                me.then(V.tensor_tensor(buf[:, :, :], xT[:, 4 * g:4 * g + 4, :], rt4(), ALU.mult))
                me.wait()
                for t in range(4):
                    k = 4 * g + t
                    ins = V.tensor_scalar(buf[:, t, :], buf[:, t, :], ga[:, k:k + 1],
                                          mod[:, 48 * l + k:48 * l + k + 1], ALU.mult, ALU.add)
                    me.then(ins)
                me.wait()
                dve.sem_inc(s_hf, 1)
                dve.wait_ge(s_yhi, n)
                V.tensor_tensor(H[:, 4 * g:4 * g + 4, S:2 * S], buf[:, :, :],
                                H[:, 4 * g:4 * g + 4, 0:S].bitcast(F32), ALU.subtract).then_inc(s_h, 1)

            V.memset(ones[:, :], 1.0).then_inc(s_tpc, 1)
            me.then(V.memset(cu[:, :, 0:2], 0.0))
            me.then(V.memset(ones_r[:, :].bitcast(F32), 1.0))
            dve.sem_inc(s_z, 4)
            dve.sem_inc(s_yr, 4)
            for i, (col, n) in enumerate(((PRM_B, 96), (PRM_PRE, 112), (PRM_CW, 96))):
                dve.wait_ge(s_tp, i + 1)
                ins = V.tensor_copy(prm[:, col:col + n], Z[i][:, 0:n])
                if i < 2:
                    ins.then_inc(s_tpc, 1)
                else:
                    ins.then_inc(s_tpc, 1)
            for g in range(GROUPS):
                for i in range(2):
                    dve.wait_ge(s_tp, 3 + 2 * g + i + 1)
                    ins = V.tensor_copy(xT[:, 4 * g + 2 * i:4 * g + 2 * i + 2, :],
                                        (SC, IN)[g % 2][i][:, :].rearrange("p (t s) -> p t s", t=2))
                    if i == 0:
                        me.then(ins)
                    else:
                        me.wait()
                        ins.then_inc(s_xn, 1)
            dve.wait_ge(s_xsum, KT)
            rstd(1, [SC[0][:, 0:S]])
            dve.wait_ge(s_cs, 1)
            pos = 0
            for g in range(GROUPS):
                for part in (1, 0):
                    k = 2 * g + (1 - part)
                    for kc in range(GROUPS):
                        ada_chunk(pos % SLOTS, 16 * (pos // SLOTS + 1), kc)
                        pos += 1
                    dve.sem_inc(s_acc, 1)
                    ada_low(k)
                    mods(k, KT * part + 4 * g)
                dve.wait_ge(s_mod, 2 * g + 2)
                h_group(0, g, g + 1)

            yhi_layer = TURNS + GROUPS + GROUPS
            for l in range(LAYERS):
                yhi0 = GROUPS + l * (TURNS + GROUPS + GROUPS)
                before = ada_before(l)
                span = CH_TURN + ADA_TURN[l] * GROUPS
                if l == 0:
                    p0 = stage_pos(l, 0, 0)
                    split(p0 % SLOTS, 0, 0, 0)
                    used()
                with dve.Fori(0, TURNS) as j:
                    me.loop(j, PER_TURN[l])
                    seen = 0
                    for w in range(1, CH_TURN + 1):
                        for i in range(before[w]):
                            rel = stage_pos(l, 0, w) - before[w] + i
                            ada_chunk(rel % SLOTS, j * (16 * span // SLOTS) + 16 * (rel // SLOTS + 1), seen % GROUPS)
                            seen += 1
                            if seen % GROUPS == 0:
                                dve.sem_inc(s_acc, 1)
                                ada_low(ada_no(l, j, seen // GROUPS - 1))
                        rel = stage_pos(l, 0, w)
                        split(rel % SLOTS, 0, w % 2, ck(l, j, w))
                        used()
                        if w % GROUPS:
                            continue
                        b = w // GROUPS - 1
                        dst = {QK: bufA, GR: sg, GC: bufB, UU: bufA, GB: bufB, GG: bufA}.get(b)
                        if b == VV:
                            for i in range(NT):
                                dve.wait_ge(s_pe, 8 + 4 * ck(l, j, w - 1) + 2 * i + 2)
                                V.tensor_copy(v_sb[:, i, :], Z[i][:, :]).then_inc(s_z, 1)
                            for h in range(2):
                                dve.wait_ge(s_sc, 2 * TURNS * l + h + 1 + 2 * j)
                                if h == 0:
                                    dve.wait_ge(s_dec, 16 * (TURNS * l + 1) + 16 * j)
                                V.tensor_tensor(p_sb[:, h, 0:S], SC[h][:, 0:S], dec[:, h, :], ALU.mult)
                                V.tensor_tensor(p_sb[:, h, S:S + P], SC[h][:, S:S + P], dec[:, h, 0:P], ALU.mult)\
                                    .then_inc(s_p, 1)
                        else:
                            if b == GB:
                                dve.wait_ge(s_cu, TURNS * l + 1 + j)
                            for t in range(TILES):
                                z_out_of(t, zlo_at(l, j, b) + t + 1, dst[:, t, :])
                        if b == GR:
                            for h in range(2):
                                dve.wait_ge(s_in, 2 * TURNS * l + h + 1 + 2 * j)
                                for i in range(NT):
                                    me.then(V.bn_stats(stats[:, 2 * h + i, :], IN[h][:, i * DV:(i + 1) * DV]))
                            me.wait()
                            hold(dve, "dve")
                            for q in range(4):
                                ins = V.bn_aggr(mv[:, q, :], stats[:, q, :])
                            ins.then_inc(s_mv, 1)
                            dve.wait_ge(s_rs, TURNS * l + 1 + j)
                            for q in range(4):
                                ins = V.tensor_scalar(bufC[:, q, :], IN[q // 2][:, (q % 2) * DV:(q % 2 + 1) * DV],
                                                      mv[:, q, 0:1], rs4[:, q:q + 1], ALU.subtract, ALU.mult)
                            ins.then_inc(s_yn, 1)
                        if b == GC:
                            dve.wait_ge(s_sgr, TURNS * l + 1 + j)
                            for q in range(4):
                                if q % 2 == 0:
                                    dve.wait_ge(s_tr, 2 * TURNS * l + q // 2 + 1 + 2 * j)
                                V.scalar_tensor_tensor(
                                    yr[:, bass.ds(j * 4 + q, 1), :].rearrange("p o s -> p (o s)"),
                                    SC[q // 2][:, (q % 2) * S:(q % 2 + 1) * S],
                                    prm[:, bass.ds(j * 4 + PRM_GN + KT * l + q, 1)], sg[:, q, :],
                                    ALU.mult, ALU.mult).then_inc(s_yr, 1)
                        if b == GB:
                            for k in range(CONV_K):
                                if k:
                                    me.wait()
                                for t in range(TILES):
                                    wk = prm[:, bass.ds(j * 4 + PRM_CW + 48 * l + KT * k + t, 1)]
                                    if k == 0:
                                        me.then(V.tensor_scalar(bufC[:, t, :], cu[:, t, 0:S], wk, None, ALU.mult))
                                    else:
                                        me.then(V.scalar_tensor_tensor(bufC[:, t, :], cu[:, t, k:k + S], wk,
                                                                       bufC[:, t, :], ALU.mult, ALU.add))
                            me.wait()
                            dve.sem_inc(s_cv, 1)
                        if b == GG:
                            dve.wait_ge(s_sg, TURNS * l + 1 + j)
                            dve.wait_ge(s_cg, TURNS * l + 1 + j)
                            V.tensor_tensor(bufC[:, :, :], bufC[:, :, :], bufA[:, :, :], ALU.mult).then_inc(s_y, 1)
                            dve.wait_ge(s_yhi, yhi0 + 1 + j)
                            V.tensor_tensor(Y2[:, bass.ds(j * 4, 4), S:2 * S], bufC[:, :, :],
                                            Y2[:, bass.ds(j * 4, 4), 0:S].bitcast(F32), ALU.subtract).then_inc(s_y2, 1)
                        if b in mod_points(l):
                            m = mod_points(l).index(b)
                            al, part = ADA_WHAT[l][m]
                            mods(ada_no(l, j, m), j * 4 + 48 * al + KT * part)
                    me.end(TURNS)

                def out_block(nb, first=False, last=False):
                    for w in range(1, OUT_CH + (0 if last else 1)):
                        split(w % SLOTS, 0, w % 2, ck_out(l, nb, w))
                        used()
                        if first and w <= GROUPS:
                            dve.wait_ge(s_yhi, yhi0 + TURNS + w)
                            V.tensor_tensor(H[:, 4 * w - 4:4 * w, S:2 * S], yr[:, 4 * w - 4:4 * w, :],
                                            H[:, 4 * w - 4:4 * w, 0:S].bitcast(F32), ALU.subtract).then_inc(s_hr, 1)
                    for t in range(TILES):
                        z_out_of(t, zlo_out(l, nb) + t + 1,
                                 yr[:, bass.ds(nb * 4 + t, 1), :].rearrange("p o s -> p (o s)"))

                dve.wait_ge(s_yr, 4 + 4 * TURNS * (l + 1))
                out_block(0, first=True)
                with dve.Fori(1, 3) as nb:
                    out_block(nb)
                out_block(3, last=l == LAYERS - 1)
                dve.wait_ge(s_mod, ada_no(l, TURNS, 0))
                me.then(V.tensor_tensor(gp[:, :], mod[:, 48 * l + 2 * KT:48 * l + 3 * KT],
                                        prm[:, PRM_POST + KT * l:PRM_POST + KT * l + KT], ALU.mult))
                dve.wait_ge(s_osum, KT * (l + 1))
                rstd(2 * l + 2, [IN[0][:, 0:S], IN[0][:, S:2 * S], IN[1][:, 0:S], IN[1][:, S:2 * S]])
                for g in range(GROUPS):
                    me.then(V.tensor_tensor(yr[:, 4 * g:4 * g + 4, :], yr[:, 4 * g:4 * g + 4, :], rt4(), ALU.mult))
                    me.wait()
                    for t in range(4):
                        k = 4 * g + t
                        me.then(V.scalar_tensor_tensor(xT[:, k, :], yr[:, k, :], gp[:, k:k + 1], xT[:, k, :],
                                                       ALU.mult, ALU.add))
                    me.wait()
                    dve.sem_inc(s_xn, 1)
                if l < LAYERS - 1:
                    dve.wait_ge(s_xsum, KT * (l + 2))
                    rstd(2 * l + 3, [SC[0][:, 0:S]])
                    for g in range(GROUPS):
                        h_group(l + 1, g, yhi0 + TURNS + GROUPS + g + 1)
            for g in range(GROUPS):
                dve.wait_ge(s_ot, 2 * g + 1)
                V.tensor_copy(stage[:, 0, g, :], (SC, IN)[g % 2][0][:, :]).then_inc(s_oc[0], 1)

        @block.gpsimd
        def _(pool):
            me = Steps(pool, s_pd)
            G = nc.gpsimd

            def step(ins):
                me.then(ins)
                me.wait()

            step(G.memset(mhalf[:, :], -0.5))
            ang, u, n = bufC[:, 1, :], bufC[:, 2, :], bufC[:, 3, :]
            pool.wait_ge(s_pos, 16)
            pool.wait_ge(s_par, 16 * 12)
            step(G.tensor_copy(u, bufC[:, 0, :].bitcast(I32)))
            step(G.tensor_scalar(ang, u, ident[:, P:P + 1], None, ALU.mult))
            turn = 2 * math.pi
            c1 = round(turn * 2 ** 9) / 2 ** 9
            c2 = round((turn - c1) * 2 ** 21) / 2 ** 21
            c3 = turn - c1 - c2
            whole = 1.5 * 2 ** 23
            for scale in (2.0 ** 20, 2.0 ** 10, 1.0):
                step(G.tensor_scalar(n, ang, 1.0 / (turn * scale), None, ALU.mult))
                step(G.tensor_scalar(n, n, whole, None, ALU.add))
                step(G.tensor_scalar(n, n, whole, None, ALU.subtract))
                for part in (c1, c2, c3):
                    step(G.tensor_scalar(u, n, part * scale, None, ALU.mult))
                    step(G.tensor_tensor(ang, ang, u, ALU.subtract))
            edge = float(np.nextafter(np.float32(math.pi), np.float32(0)))
            step(G.tensor_scalar(ang, ang, edge, None, ALU.min))
            step(G.tensor_scalar(ang, ang, -edge, None, ALU.max))
            pool.sem_inc(s_tab, 1)
            pool.wait_ge(s_sin, 2)
            step(G.tensor_tensor(cos_t[:, :], cos_t[:, :], cos_t[:, :], ALU.mult))
            step(G.tensor_scalar(cos_t[:, :], cos_t[:, :], -2.0, 1.0, ALU.mult, ALU.add))
            step(G.tensor_scalar(sin_t[:, :], sin_t[:, :], ident[:, P + 1:P + 2], None, ALU.mult))

            def all4(t):
                return t[:, :].rearrange("p (o s) -> p o s", o=1).broadcast_to([P, 4, S])

            for l in range(LAYERS):
                with pool.Fori(0, TURNS) as j:
                    me.loop(j, 3)
                    pool.wait_ge(s_z, z_at(l, j, VV))
                    me.then(G.tensor_tensor(bufC[:, :, :], bufA[:, :, :], all4(cos_t), ALU.mult))
                    pool.wait_ge(s_swap, 2 * TURNS * l + 2 + 2 * j)
                    me.then(G.tensor_tensor(bufB[:, :, :], bufB[:, :, :], all4(sin_t), ALU.mult))
                    me.wait()
                    G.tensor_tensor(bufC[:, :, :], bufC[:, :, :], bufB[:, :, :], ALU.add).then_inc(s_rope, 1)
                    pool.wait_ge(s_mv, TURNS * l + 1 + j)
                    hold(pool, "pool")
                    me.then(G.tensor_scalar(rs4[:, :], mv[:, :, 1], EPS, None, ALU.add))
                    me.wait()
                    G.tensor_tensor(rs4[:, :], rs4[:, :], mhalf[:, :], ALU.pow).then_inc(s_rs, 1)
                    pool.wait_ge(s_z, z_at(l, j, GB))
                    G.tensor_tensor(cu[:, :, 2:S + 2], bufA[:, :, :], bufB[:, :, :], ALU.mult).then_inc(s_cu, 1)
                    pool.wait_ge(s_cv, TURNS * l + 1 + j)
                    G.tensor_tensor(bufC[:, :, :], bufC[:, :, :], bufB[:, :, :], ALU.mult).then_inc(s_cg, 1)
                    me.end(TURNS)

        @block.tensor
        def _(pe):
            T = nc.tensor
            I = ident[:, 0:P]

            def chunk(parity, n, kc, rhs, z, nk=GROUPS, ready=None):
                for t in range(TILES):
                    if kc == 0:
                        pe.wait_ge(s_z, z(t))
                    for a in range(CK):
                        if t == 0 and a % 2 == 0:
                            pe.wait_ge(s_lo, 2 * n + a // 2 + 1)
                        wh = w_hi[:, 2 * parity + a // 2, a % 2, t * P:(t + 1) * P]
                        wl = w_lo[:, 2 * parity + a // 2, a % 2, t * P:(t + 1) * P]
                        act = rhs(CK * kc + a)
                        start = kc == 0 and a == 0
                        stop = kc == nk - 1 and a == CK - 1
                        if start:
                            T.matmul(Z[t][:, :], wh, act, start=True, stop=False)
                        ins = T.matmul(Z[t][:, 0:S], wl, act[:, 0:S], start=False, stop=False)
                        if not start:
                            ins = T.matmul(Z[t][:, :], wh, act, start=False, stop=stop)
                    ins.then_inc(s_pe, 1)

            def v_chunk(parity, n, kc, z):
                for i in range(NT):
                    if kc == 0:
                        pe.wait_ge(s_z, z(i))
                    for a in range(CK):
                        if i == 0 and a % 2 == 0:
                            pe.wait_ge(s_lo, 2 * n + a // 2 + 1)
                        wh = w_hi[:, 2 * parity + a // 2, a % 2, :]
                        wl = w_lo[:, 2 * parity + a // 2, a % 2, :]
                        hh = H[:, CK * kc + a, i * P:(i + 1) * P]
                        hl = H[:, CK * kc + a, S + i * P:S + (i + 1) * P]
                        T.matmul(Z[i][:, :], hh, wh, start=kc == 0 and a == 0, stop=False)
                        T.matmul(Z[i][:, :], hh, wl, start=False, stop=False)
                        ins = T.matmul(Z[i][:, :], hl, wh, start=False,
                                       stop=kc == GROUPS - 1 and a == CK - 1)
                    ins.then_inc(s_pe, 2)

            def ada_sum(k):
                pe.wait_ge(s_alo, k + 1)
                for t in range(TILES):
                    T.matmul(IN[1][:, 2 * t:2 * t + 2], acc_hi[:, t * P:(t + 1) * P], ones_r[:, :], start=True, stop=False)
                    ins = T.matmul(IN[1][:, 2 * t:2 * t + 2], acc_lo[:, t * P:(t + 1) * P], ones_r[:, :], start=False, stop=True)
                ins.then_inc(s_mm, 1)

            def x_sum(k):
                for g in range(GROUPS):
                    pe.wait_ge(s_xsq, GROUPS * k + g + 1)
                    for t in range(4):
                        T.matmul(SC[0][:, 0:S], ones[:, :], (bufA, bufB)[g % 2][:, t, :], start=g == 0 and t == 0,
                                 stop=g == 3 and t == 3).then_inc(s_xsum, 1)

            pe.wait_ge(s_par, 16 * 12)
            for i, n in enumerate((96, 112, 96)):
                T.transpose(Z[i][:, 0:n], bufA[0:n, i, 0:P], ident[0:n, 0:n]).then_inc(s_tp, 1)
            pe.wait_ge(s_x, 32)
            rows = yr[:, :, :].rearrange("p t s -> p (t s)")
            for g in range(GROUPS):
                if g >= 2:
                    pe.wait_ge(s_xn, g - 1)
                for i in range(2):
                    for q in range(2):
                        for tok in range(NT):
                            col = tok * D + (4 * g + 2 * i + q) * P
                            ins = T.transpose((SC, IN)[g % 2][i][:, q * S + tok * P:q * S + (tok + 1) * P],
                                              rows[:, col:col + P], I)
                    ins.then_inc(s_tp, 1)
            pe.wait_ge(s_xn, 4)
            x_sum(0)
            for g in range(GROUPS):
                for i in range(2):
                    if g or i:
                        pe.wait_ge(s_mod, 2 * g + i)
                    ada_sum(2 * g + i)
            pe.sem_inc(s_pe, 8)

            for l in range(LAYERS):
                with pe.Fori(0, TURNS) as j:
                    for b in range(BLOCKS):
                        pb = b - 1 if b else GG
                        z0 = z_at(l, j, b) - (2 if pb == VV else 4)
                        for kc in range(GROUPS):
                            w = GROUPS * b + kc
                            if b == QK:
                                pe.wait_ge(s_h, GROUPS * l + kc + 1)
                            z = lambda t: z0 + min(t + 1, 2 if pb == VV else 4)
                            if b == VV:
                                v_chunk(w % 2, ck(l, j, w), kc, z)
                            else:
                                chunk(w % 2, ck(l, j, w), kc, lambda k: H[:, k, :], z)
                        if b == VV:
                            pe.wait_ge(s_rope, TURNS * l + 1 + j)
                            pe.wait_ge(s_yr, 4 * TURNS * l + 4 + 4 * j)
                            for h in range(2):
                                q, k = bufC[:, h, :], bufC[:, 2 + h, :]
                                T.matmul(SC[h][:, 0:S], k[:, 0:P], q, start=True, stop=True)
                                T.matmul(SC[h][:, S:S + P], k[:, P:S], q[:, P:S], start=True, stop=True).then_inc(s_sc, 1)
                        if b == GR:
                            for h in range(2):
                                pe.wait_ge(s_p, 2 * TURNS * l + h + 1 + 2 * j)
                                v0, v1 = (v_sb[:, i, h * DV:(h + 1) * DV] for i in range(NT))
                                T.matmul(IN[h][:, 0:DV], p_sb[:, h, 0:P], v0, start=True, stop=True)
                                T.matmul(IN[h][:, DV:2 * DV], p_sb[:, h, P:2 * P], v0, start=True, stop=False)
                                T.matmul(IN[h][:, DV:2 * DV], p_sb[:, h, 2 * P:3 * P], v1, start=False, stop=True)\
                                    .then_inc(s_in, 1)
                        if b == GC:
                            pe.wait_ge(s_yn, TURNS * l + 1 + j)
                            for h in range(2):
                                for e in range(2):
                                    for i in range(NT):
                                        ins = T.transpose(SC[h][:, e * S + i * P:e * S + (i + 1) * P],
                                                          bufC[:, 2 * h + i, e * P:(e + 1) * P], I)
                                ins.then_inc(s_tr, 1)
                        if b in mod_points(l):
                            ada_sum(ada_no(l, j, mod_points(l).index(b)))

                def o_sum(nb):
                    pe.wait_ge(s_o, KT * l + 4 + 4 * nb)
                    for t in range(4):
                        dst = (IN[nb // 2][:, (nb % 2) * S:(nb % 2 + 1) * S])
                        T.matmul(dst, ones[:, :], bufA[:, t, :], start=t == 0, stop=t == 3).then_inc(s_osum, 1)

                def src(k):
                    return Y2[:, k, :] if k < KT else H[:, k - KT, :]

                for nb in range(D // BLK):
                    for w in range(OUT_CH):
                        if nb == 0:
                            if w < GROUPS:
                                pe.wait_ge(s_y2, TURNS * l + w + 1)
                            else:
                                pe.wait_ge(s_hr, GROUPS * l + w - GROUPS + 1)
                        chunk(w % 2, ck_out(l, nb, w), w, src, lambda t: z_out(l, nb) - 4 + t + 1, nk=OUT_CH)
                        if w == 1 and nb:
                            if nb == 1:
                                pe.wait_ge(s_mod, ada_no(l, TURNS, 0))
                            o_sum(nb - 1)
                o_sum(D // BLK - 1)
                if l < LAYERS - 1:
                    x_sum(l + 1)
            for g in range(GROUPS):
                pe.wait_ge(s_xn, GROUPS * LAYERS + g + 1)
                if g >= 2:
                    pe.wait_ge(s_oc[0], g - 1)
                    pe.wait_ge(s_oc[1], g - 1)
                for i in range(NT):
                    for t in range(4):
                        ins = T.transpose((SC, IN)[g % 2][i][:, t * P:(t + 1) * P],
                                          xT[:, 4 * g + t, i * P:(i + 1) * P], I)
                    ins.then_inc(s_ot, 1)


PER_TURN = [ADA_TURN[l] * GROUPS * CK + 4 + CONV_K * TILES for l in range(LAYERS)]


def constants():
    half = DK // 2
    f = (np.float32(10000.0) ** (-np.arange(half, dtype=np.float32) / np.float32(half))).astype(np.float32)
    cst = np.zeros((P, P + 2), np.float32)
    cst[:, :P] = np.eye(P, dtype=np.float32)
    cst[:, P] = np.concatenate([f, f])
    cst[:, P + 1] = np.concatenate([-np.ones(half), np.ones(half)])
    gamma = 1.0 - 2.0 ** (-5.0 - np.arange(HEADS))
    diff = np.arange(S)[None, :] - np.arange(P)[:, None]
    dec = np.where(diff[None] >= 0, gamma[:, None, None] ** np.maximum(diff, 0)[None], 0.0) * DK ** -0.5
    dec = dec.reshape(TURNS, 2, P, S).transpose(0, 2, 1, 3)
    dec = np.concatenate([dec, dec[:1]])
    return cst, np.ascontiguousarray(dec.astype(np.float32))


_INS = ["x", "c", "positions", "norm_pre", "norm_post", "w_ada", "b_ada", "w_in", "conv_w", "gn_gain", "w_out"]


def kernel(**inputs):
    import concourse.bacc as bacc
    from concourse.bass_utils import run_bass_kernel_spmd

    nc = bacc.Bacc("TRN2", target_bir_lowering=False, num_devices=1)
    arrays, args = {}, []
    for name in _INS:
        a = np.ascontiguousarray(inputs[name])
        arrays[f"in_{name}"] = a
        args.append(nc.dram_tensor(f"in_{name}", a.shape, mybir.dt.from_np(a.dtype), kind="ExternalInput").ap())
    for name, a in zip(("consts", "decay"), constants()):
        arrays[name] = a
        args.append(nc.dram_tensor(name, a.shape, F32, kind="ExternalInput").ap())
    args.append(nc.dram_tensor("out", (1, S, D), F32, kind="ExternalOutput").ap())
    build(nc, *args)
    r = run_bass_kernel_spmd(nc, [arrays], core_ids=[0])
    return r.results[0]["out"]
```

```python
import math
from contextlib import ExitStack

import numpy as np

import concourse.bass as bass
from concourse import mybir

F32 = mybir.dt.float32
F32R = mybir.dt.float32r
I32 = mybir.dt.int32
ALU = mybir.AluOpType
ACT = mybir.ActivationFunctionType

P = 128
D = 2048
S = 256
LAYERS = 2
KT = D // P
NT = S // P
W_CONV = 2048
HEADS = 8
DK, DV = 128, 256
W_QK = HEADS * DK
CONV_K = 3
EPS = 1e-6
COL_GB, COL_GC, COL_U, COL_G = 0, W_CONV, 2 * W_CONV, 3 * W_CONV
COL_Q = 4 * W_CONV
COL_V = COL_Q + 2 * W_QK
COL_GR = COL_V + HEADS * DV
BLK = 512
TILES = BLK // P
CK = 4
GROUPS = KT // CK
SLOTS = 4
QK, VV, GC, UU, GB, GG, GR = range(7)
BLOCKS = 7
TURNS = 4
CH_TURN = BLOCKS * GROUPS
CH_OUT = (2 * D // (CK * P)) * (D // BLK)
OUT_CH = 2 * D // (CK * P)
CH_LAYER = TURNS * CH_TURN + CH_OUT
LEAD = 4
COL = 32
ADA_START = 8
ADA_TURN = (3, 1)
Z_TURN = 26
Z_OUT = D // P
Z_LAYER = TURNS * Z_TURN + Z_OUT
LO_TURN = 24
LO_LAYER = TURNS * LO_TURN + Z_OUT
PRM_B, PRM_PRE, PRM_POST, PRM_GN, PRM_C, PRM_CW = 0, 96, 128, 160, 192, 208
PRM = 304


def ada_before(layer):
    n = ADA_TURN[layer] * GROUPS
    at = [0] * (CH_TURN + LEAD)
    for i in range(n):
        at[LEAD + 1 + (i * (CH_TURN - LEAD)) // n] += 1
    return at


def mod_points(layer):
    return (GC, GB, GR) if layer == 0 else (GR,)


def build(nc, x, c, positions, norm_pre, norm_post, w_ada, b_ada, w_in, conv_w, gn_gain, w_out,
          consts, decay, out):
    ctx = ExitStack()
    with ctx:
        def sb(name, shape, dt=F32):
            return ctx.enter_context(nc.sbuf_tensor(name, shape, dt))

        def sem(name):
            return ctx.enter_context(nc.semaphore(name))

        xT = sb("xT", [P, KT, S])
        H = sb("H", [P, KT, 2 * S], F32R)
        Y2 = sb("Y2", [P, KT, 2 * S], F32R)
        yr = sb("yr", [P, KT, S])
        stage = sb("stage", [P, SLOTS, CK, BLK])
        w_hi = sb("w_hi", [P, 4, 2, BLK], F32R)
        w_lo = sb("w_lo", [P, 4, 2, BLK], F32R)
        bufA = sb("bufA", [P, 4, S])
        bufB = sb("bufB", [P, 4, S])
        bufC = sb("bufC", [P, 4, S])
        cu = sb("cu", [P, 4, S + 2])
        v_sb = sb("v_sb", [P, NT, 2 * DV])
        sg = sb("sg", [P, 4, S])
        p_sb = sb("p_sb", [P, 2, 3 * P])
        lo_sb = sb("lo_sb", [P, 2, S])
        dec = sb("dec", [P, 2, S])
        cos_t = sb("cos_t", [P, S])
        sin_t = sb("sin_t", [P, S])
        acc = sb("acc", [P, BLK])
        acc_hi = sb("acc_hi", [P, BLK], F32R)
        acc_lo = sb("acc_lo", [P, BLK], F32R)
        ident = sb("ident", [P, P + 2])
        ones = sb("ones", [P, P])
        ones_r = sb("ones_r", [P, 2], F32R)
        prm = sb("prm", [P, PRM])
        mod = sb("mod", [P, LAYERS * 3 * KT])
        c_silu = sb("c_silu", [P, KT])
        c_cols = sb("c_cols", [P, KT, COL])
        ga = sb("ga", [P, KT])
        gp = sb("gp", [P, KT])
        stats = sb("stats", [P, 4, 6])
        mv = sb("mv", [P, 4, 2])
        rs4 = sb("rs4", [P, 4])
        nb4 = sb("nb4", [P, 4])
        mhalf = sb("mhalf", [P, 4])
        var_t, rt, tmp_t = (cu[:, t, 2:S + 2] for t in range(3))

        Z = [ctx.enter_context(nc.psum_tensor(f"Z{t}", [P, 2 * S], F32)) for t in range(4)]
        SC = [ctx.enter_context(nc.psum_tensor(f"SC{t}", [P, 2 * S], F32)) for t in range(2)]
        IN = [ctx.enter_context(nc.psum_tensor(f"IN{t}", [P, 2 * S], F32)) for t in range(2)]

        s_par = sem("params_loaded")
        s_x = sem("x_loaded")
        s_pos = sem("positions_loaded")
        s_dec = sem("decay_loaded")
        s_stage = [sem(f"stage_loaded{i}") for i in range(SLOTS)]
        s_k = [sem(f"k_columns_loaded{i}") for i in range(GROUPS)]
        s_used = sem("stage_used")
        s_hi = sem("hi_done")
        s_lo = sem("lo_done")
        s_pe = sem("pe_tiles")
        s_zlo = sem("z_lo_copied")
        s_z = sem("z_free")
        s_swap = sem("qk_swapped")
        s_rope = sem("rope_done")
        s_sgr = sem("silu_gr_done")
        s_sc = sem("scores_done")
        s_p = sem("p_done")
        s_in = sem("inner_done")
        s_mv = sem("head_stats_done")
        s_rs = sem("head_rstd_done")
        s_yn = sem("heads_normalised")
        s_tr = sem("heads_transposed")
        s_yr = sem("yret_done")
        s_cu = sem("cu_done")
        s_cv = sem("conv_done")
        s_cg = sem("conv_gated")
        s_sg = sem("silu_g_done")
        s_y = sem("yconv_done")
        s_yhi = sem("y_hi_done")
        s_y2 = sem("yconv_split")
        s_hr = sem("yret_split")
        s_acc = sem("ada_acc_done")
        s_ahi = sem("ada_hi_done")
        s_alo = sem("ada_lo_done")
        s_mm = sem("ada_summed")
        s_mod = sem("mod_done")
        s_o = sem("o_squared")
        s_osum = sem("o_summed")
        s_xn = sem("x_new")
        s_xsq = sem("x_squared")
        s_xsum = sem("x_summed")
        s_var = sem("variance_done")
        s_adapart = sem("ada_chunk_multiplied")
        s_sqrt = sem("sqrt_done")
        s_hf = sem("h_done")
        s_h = sem("h_split")
        s_tp = sem("start_transposes")
        s_tpc = sem("start_copied")
        s_cs = sem("c_silu_done")
        s_tab = sem("angle_done")
        s_xc = sem("x_copied")
        s_sin = sem("sines_done")
        s_rot = sem("tables_done")
        s_ot = sem("out_transposed")
        s_oc = [sem("out_copied_v"), sem("out_copied_s")]
        s_out = sem("out_stored")
        s_vd = sem("vector_step")
        s_pd = sem("pool_step")
        s_ad = sem("scalar_step")

        s_held = {e: sem(f"{e}_held") for e in ("sp", "dve", "pool")}

        block = ctx.enter_context(nc.Block())

        def hold(eng, name):
            eng.sem_inc(s_held[name], 1)

        class Steps:

            def __init__(self, eng, s):
                self.eng, self.s, self.n, self.turn, self.per = eng, s, 0, None, 0

            def then(self, ins):
                ins.then_inc(self.s, 1)
                self.n += 1
                self.last = self.n if self.turn is None else self.n + self.turn * self.per

            def wait(self):
                self.eng.wait_ge(self.s, self.last)

            def loop(self, turn, per):
                self.turn, self.per, self.at = turn, per, self.n

            def end(self, turns):
                assert self.n - self.at == self.per, (self.n - self.at, self.per)
                self.n += self.per * (turns - 1)
                self.turn = None

        def stage_pos(layer, j, w):
            base = ADA_START * GROUPS
            for earlier in range(layer):
                base += TURNS * (CH_TURN + ADA_TURN[earlier] * GROUPS) + CH_OUT
            return base + w + sum(ada_before(layer)[:w + 1]) + j * (CH_TURN + ADA_TURN[layer] * GROUPS)

        def out_pos(layer, nb, w):
            return stage_pos(layer, TURNS, 0) + OUT_CH * nb + w

        def ck(layer, j, w):
            return CH_LAYER * layer + w + j * CH_TURN

        def ck_out(layer, nb, w):
            return CH_LAYER * layer + TURNS * CH_TURN + w + nb * OUT_CH

        def z_at(layer, j, b):
            return 4 + Z_LAYER * layer + 4 * b - (2 if b > VV else 0) + j * Z_TURN

        def zlo_at(layer, j, b):
            return LO_LAYER * layer + 4 * b - (4 if b > VV else 0) + j * LO_TURN

        def z_out(layer, nb):
            return 4 + Z_LAYER * layer + TURNS * Z_TURN + nb * 4

        def zlo_out(layer, nb):
            return LO_LAYER * layer + TURNS * LO_TURN + nb * 4

        def ada_no(layer, j, m):
            return ADA_START + (TURNS * ADA_TURN[0] if layer else 0) + m + j * ADA_TURN[layer]

        def ada_bank(b):
            return SC[1] if b == GC else IN[1]

        ADA_WHAT = (((0, 2), (1, 1), (1, 0)), ((1, 2),))

        @block.sync
        def _(sp):
            def load(slot, pos, dst, src, first=False):
                if not first:
                    sp.wait_ge(s_used, pos - SLOTS + 1)
                    hold(sp, "sp")
                sp.dma_start(dst, src).then_inc(s_stage[slot], 16)

            def rows(w, kc):
                return w[kc * CK * P:(kc + 1) * CK * P, :].rearrange("(a p) n -> p a n", p=P)

            sp.dma_start(ident[:, :], consts).then_inc(s_par, 16)
            pr = yr[:, :, :].rearrange("p t s -> p (t s)")
            for l in range(LAYERS):
                sp.dma_start(bufA[48 * l:48 * l + 48, 0, 0:P],
                             b_ada[l, :].rearrange("(r q) -> r q", q=P)).then_inc(s_par, 16)
                for i, g in enumerate((norm_pre, norm_post, gn_gain)):
                    r = 32 * i + 16 * l
                    sp.dma_start(bufA[r:r + 16, 1, 0:P],
                                 g[l, :].rearrange("(r q) -> r q", q=P)).then_inc(s_par, 16)
                sp.dma_start(bufA[48 * l:48 * l + 48, 2, 0:P],
                             conv_w[l, :, :].rearrange("k (r q) -> (k r) q", q=P)).then_inc(s_par, 16)
            sp.dma_start(bufA[96:112, 1, 0:P], c[0, :].rearrange("(r q) -> r q", q=P)).then_inc(s_par, 16)
            pos = 0
            for g in range(GROUPS):
                for part in (1, 0):
                    for kc in range(GROUPS):
                        col = part * D + g * BLK
                        if pos >= SLOTS:
                            sp.wait_ge(s_adapart, pos - SLOTS + 1)
                        load(pos % SLOTS, pos, stage[:, pos % SLOTS, :, :],
                             rows(w_ada[0, :, :], kc)[:, :, col:col + BLK], first=True)
                        if pos == SLOTS - 1:
                            for i in range(NT):
                                sp.dma_start(pr[:, i * D:(i + 1) * D], x[0, i * P:(i + 1) * P, :]).then_inc(s_x, 16)
                        pos += 1
            sp.wait_ge(s_adapart, GROUPS * ADA_START)
            sp.dma_start(dec[:, :, :], decay[0, :, :, :]).then_inc(s_dec, 16)
            for l in range(LAYERS):
                before = ada_before(l)
                with sp.Fori(0, TURNS) as j:
                    slot0 = stage_pos(l, 0, 0) % SLOTS
                    assert slot0 == 0
                    ada = 0
                    for w in range(CH_TURN):
                        for i in range(before[w]):
                            al, part = ADA_WHAT[l][ada // GROUPS]
                            rel = stage_pos(l, 0, w) - before[w] + i
                            p = stage_pos(l, j, w) - before[w] + i
                            load(rel % SLOTS, p, stage[:, rel % SLOTS, :, :],
                                 rows(w_ada[al, :, :], ada % GROUPS)[:, :, bass.ds(j * BLK + part * D, BLK)])
                            ada += 1
                        rel, p = stage_pos(l, 0, w), stage_pos(l, j, w)
                        b, kc = divmod(w, GROUPS)
                        dst = stage[:, rel % SLOTS, :, :]
                        src = rows(w_in[l, :, :], kc)
                        if b == QK:
                            sp.wait_ge(s_used, p - SLOTS + 1)
                            hold(sp, "sp")
                            sp.dma_start(dst[:, :, 0:2 * DK], src[:, :, bass.ds(j * 2 * DK + COL_Q, 2 * DK)])\
                                .then_inc(s_stage[rel % SLOTS], 16)
                            sp.dma_start(dst[:, :, 2 * DK:], src[:, :, bass.ds(j * 2 * DK + COL_Q + W_QK, 2 * DK)])\
                                .then_inc(s_k[kc], 16)
                        else:
                            col = {VV: COL_V, GR: COL_GR, GC: COL_GC, UU: COL_U, GB: COL_GB, GG: COL_G}[b]
                            load(rel % SLOTS, p, dst, src[:, :, bass.ds(j * BLK + col, BLK)])
                        if w == CH_TURN - 4:
                            sp.wait_ge(s_p, 2 * TURNS * l + 2 + 2 * j)
                            hold(sp, "sp")
                            sp.dma_start(dec[:, :, :], decay[bass.ds(j + 1, 1), :, :, :]
                                         .rearrange("o p h s -> p (o h) s")).then_inc(s_dec, 16)
                for kc in range(GROUPS):
                    sp.sem_inc(s_k[kc], 16)
                with sp.Fori(0, D // BLK) as nb:
                    for w in range(OUT_CH):
                        load(w % SLOTS, out_pos(l, nb, w), stage[:, w % SLOTS, :, :],
                             rows(w_out[l, :, :], w)[:, :, bass.ds(nb * BLK, BLK)])
            for g in range(GROUPS):
                for i in range(NT):
                    sp.wait_ge(s_oc[i], g + 1)
                    sp.dma_start(out[0, i * P:(i + 1) * P, g * BLK:(g + 1) * BLK],
                                 stage[:, i, g, :]).then_inc(s_out, 16)
            sp.wait_ge(s_out, 16 * GROUPS * NT)

        @block.scalar
        def _(act):
            def split(slot, value, w, n, block=GROUPS):
                parity = w % 2
                act.wait_ge(s_stage[slot], value)
                for h in range(2):
                    act.wait_ge(s_pe, 4 * n + (4 if h or w % block == 1 else 2))
                    nc.scalar.copy(w_hi[:, 2 * parity + h, :, :],
                                   stage[:, slot, 2 * h:2 * h + 2, :]).then_inc(s_hi, 1)

            def z_low(pe, t, zlo, z):
                act.wait_ge(s_pe, pe)
                act.wait_ge(s_z, z)
                nc.scalar.copy(lo_sb[:, t % 2, :], Z[t][:, S:2 * S]).then_inc(s_zlo, 1)

            def ada_hi(k):
                act.wait_ge(s_acc, k + 1)
                act.wait_ge(s_mm, k)
                nc.scalar.copy(acc_hi[:, :], acc[:, :]).then_inc(s_ahi, 1)

            def sqrt(k):
                act.wait_ge(s_var, k)
                nc.scalar.activation(rt, var_t, ACT.Sqrt).then_inc(s_sqrt, 1)

            def x_squares(base, k):
                for g in range(GROUPS):
                    act.wait_ge(s_xn, base + g + 1)
                    if g >= 2:
                        act.wait_ge(s_xsum, KT * k + 4 * (g - 1))
                    nc.scalar.activation((bufA, bufB)[g % 2][:, :, :], xT[:, 4 * g:4 * g + 4, :],
                                         ACT.Square).then_inc(s_xsq, 1)

            def h_hi(g, n):
                act.wait_ge(s_hf, n)
                nc.scalar.copy(H[:, 4 * g:4 * g + 4, 0:S], (bufA, bufB)[g % 2][:, :, :]).then_inc(s_yhi, 1)

            act.dma_start(bufC[:, 0, :].bitcast(I32), 
                          positions.rearrange("a s -> (a s)").partition_broadcast(P)).then_inc(s_pos, 16)
            act.wait_ge(s_tpc, 4)
            nc.scalar.activation(c_cols[:, :, 0], prm[:, PRM_C:PRM_C + KT], ACT.Silu).then_inc(s_cs, 1)
            nc.scalar.activation(c_silu[:, :], prm[:, PRM_C:PRM_C + KT], ACT.Silu).then_inc(s_cs, 1)
            for g in range(GROUPS):
                for i in range(2):
                    act.wait_ge(s_tp, 3 + 2 * g + i + 1)
                    nc.scalar.copy(xT[:, 4 * g + 2 * i:4 * g + 2 * i + 2, :],
                                   (SC, IN)[g % 2][i][:, :].rearrange("p (t s) -> p t s", t=2)).then_inc(s_xc, 1)
            act.wait_ge(s_xc, 2 * GROUPS)
            act.sem_inc(s_xn, GROUPS)
            def first_split(l, w):
                p = stage_pos(l, 0, w)
                act.wait_ge(s_k[w], 16 * ((TURNS + 1) * l + 1))
                split(p % SLOTS, 16 * (p // SLOTS + 1), w, ck(l, 0, w))

            x_squares(0, 0)
            ada_hi(0)
            ada_hi(1)
            sqrt(1)
            h_hi(0, 1)
            act.wait_ge(s_tab, 1)
            nc.scalar.activation(sin_t[:, :], bufC[:, 1, :], ACT.Sin).then_inc(s_sin, 1)
            nc.scalar.activation(cos_t[:, :], bufC[:, 1, :], ACT.Sin, scale=0.5).then_inc(s_sin, 1)
            for g in range(1, GROUPS):
                ada_hi(2 * g)
                ada_hi(2 * g + 1)
                if g == GROUPS - 1:
                    first_split(0, 0)
                h_hi(g, g + 1)

            for l in range(LAYERS):
                before = ada_before(l)
                span = CH_TURN + ADA_TURN[l] * GROUPS
                if l:
                    for g in range(GROUPS):
                        h_hi(g, GROUPS * l + g + 1)
                for w in range(1 if l == 0 else 2, LEAD):
                    first_split(l, w)
                with act.Fori(0, TURNS) as j:
                    seen = 0
                    for w in range(LEAD, CH_TURN + LEAD):
                        for _ in range(before[w]):
                            seen += 1
                            if seen % GROUPS == 0:
                                ada_hi(ada_no(l, j, seen // GROUPS - 1))
                        rel = stage_pos(l, 0, w)
                        if w >= CH_TURN:
                            act.wait_ge(s_k[w - CH_TURN], j * 16 + 16 * ((TURNS + 1) * l + 2))
                        split(rel % SLOTS, j * (16 * span // SLOTS) + 16 * (rel // SLOTS + 1), w, ck(l, j, w))
                        b = w // GROUPS - 1
                        if (b, w % GROUPS) == (GC, 3):
                            act.wait_ge(s_rs, TURNS * l + 1 + j)
                            for q in range(4):
                                ins = nc.scalar.activation(bufC[:, q, :], IN[q // 2][:, (q % 2) * DV:(q % 2 + 1) * DV],
                                                           ACT.Identity, bias=nb4[:, q:q + 1], scale=rs4[:, q:q + 1])
                            ins.then_inc(s_yn, 1)
                        if w == 4 * GG + 6:
                            act.wait_ge(s_y, TURNS * l + 1 + j)
                            nc.scalar.copy(Y2[:, bass.ds(j * 4, 4), 0:S], bufC[:, :, :]).then_inc(s_yhi, 1)
                        if w % GROUPS:
                            continue
                        if b == VV:
                            act.wait_ge(s_sc, 2 * TURNS * l + 2 + 2 * j)
                            for i in range(NT):
                                act.wait_ge(s_pe, 8 + 4 * ck(l, j, w - 1) + 2 * i + 2)
                                nc.scalar.copy(v_sb[:, i, :], Z[i][:, :]).then_inc(s_z, 1)
                        else:
                            for t in range(TILES):
                                z_low(8 + 4 * ck(l, j, w - 1) + t + 1, t, zlo_at(l, j, b), z_at(l, j, b) + max(0, t - 1))
                        if b == QK:
                            act.wait_ge(s_z, z_at(l, j, b + 1))
                            nc.scalar.copy(bufB[64:128, :, :], bufA[0:64, :, :]).then_inc(s_swap, 1)
                            nc.scalar.copy(bufB[0:64, :, :], bufA[64:128, :, :]).then_inc(s_swap, 1)
                        if b == GR:
                            act.wait_ge(s_z, z_at(l, j, b + 1))
                            nc.scalar.activation(sg[:, :, :], sg[:, :, :], ACT.Silu).then_inc(s_sgr, 1)
                        if b == GG:
                            act.wait_ge(s_z, z_at(l, j, b + 1))
                            nc.scalar.activation(bufA[:, :, :], bufA[:, :, :], ACT.Silu).then_inc(s_sg, 1)

                def out_block(nb, first=False, last=False):
                    for w in range(LEAD if first else 1, OUT_CH + (0 if last else 1)):
                        pos = out_pos(l, 0, w)
                        split(w % SLOTS, nb * (16 * OUT_CH // SLOTS) + 16 * (pos // SLOTS + 1), w,
                              ck_out(l, nb, w), OUT_CH)
                        if first and w < LEAD + GROUPS:
                            if w == LEAD:
                                act.wait_ge(s_pe, 8 + 4 * ck_out(l, 0, 0))
                                act.wait_ge(s_yr, 4 + 4 * TURNS * (l + 1))
                            q = 4 * (w - LEAD)
                            nc.scalar.copy(H[:, q:q + 4, 0:S], yr[:, q:q + 4, :]).then_inc(s_yhi, 1)
                    if not last:
                        out_z(nb, first)

                def out_z(nb, first=False):
                    for t in range(TILES):
                        z_low(8 + 4 * ck_out(l, nb, OUT_CH - 1) + t + 1, t, 0, z_out(l, nb) + max(0, t - 1))
                    if not first or l:
                        act.wait_ge(s_osum, KT * l + 4 * nb)
                    for t in range(TILES):
                        act.wait_ge(s_z, z_out(l, nb) + t + 1)
                        nc.scalar.activation(bufA[:, t, :], yr[:, bass.ds(nb * 4 + t, 1), :].rearrange("p o s -> p (o s)")
                                             if not isinstance(nb, int) else yr[:, nb * 4 + t, :],
                                             ACT.Square).then_inc(s_o, 1)

                out_block(0, first=True)
                with act.Fori(1, 3) as nb:
                    out_block(nb)
                out_block(3, last=True)
                if l < LAYERS - 1:
                    first_split(l + 1, 0)
                    out_z(3)
                    first_split(l + 1, 1)
                else:
                    out_z(3)
                sqrt(2 * l + 2)
                if l < LAYERS - 1:
                    x_squares(GROUPS * (l + 1), l + 1)
                    sqrt(2 * l + 3)
            for g in range(GROUPS):
                act.wait_ge(s_ot, 2 * g + 2)
                nc.scalar.copy(stage[:, 1, g, :], (SC, IN)[g % 2][1][:, :]).then_inc(s_oc[1], 1)

        @block.vector
        def _(dve):
            me = Steps(dve, s_vd)
            V = nc.vector

            def split(slot, parity, n):
                for h in range(2):
                    dve.wait_ge(s_hi, 2 * n + h + 1)
                    ins = V.tensor_tensor(w_lo[:, 2 * parity + h, :, :], stage[:, slot, 2 * h:2 * h + 2, :],
                                          w_hi[:, 2 * parity + h, :, :].bitcast(F32), ALU.subtract)
                    ins.then_inc(s_lo, 1)
                dve.wait_ge(s_lo, 2 * n + 2)
                used()

            def ada_chunk(slot, value, kc, first, count=1):
                dve.wait_ge(s_stage[slot], value)
                for a in range(CK):
                    k = CK * kc + a
                    w = stage[:, slot, a, :]
                    if first and a == 0:
                        ins = V.tensor_scalar(acc[:, :], w, c_silu[:, k:k + 1], None, ALU.mult)
                    else:
                        me.wait()
                        ins = V.scalar_tensor_tensor(acc[:, :], w, c_silu[:, k:k + 1], acc[:, :],
                                                     ALU.mult, ALU.add)
                    me.then(ins)
                me.wait()
                used(count)

            def ada_low(k):
                dve.wait_ge(s_ahi, k + 1)
                V.tensor_tensor(acc_lo[:, :], acc[:, :], acc_hi[:, :].bitcast(F32), ALU.subtract).then_inc(s_alo, 1)

            def used(count=1):
                dve.sem_inc(s_used, count)

            def mods(k, col, bank):
                dve.wait_ge(s_mm, k + 1)
                V.tensor_tensor(mod[:, bass.ds(col, 4)], ada_bank(bank)[:, 0:8:2], prm[:, bass.ds(col, 4)], ALU.add)\
                    .then_inc(s_mod, 1)

            def z_out_of(t, zlo, dst):
                dve.wait_ge(s_zlo, zlo)
                V.tensor_tensor(dst, Z[t][:, 0:S], lo_sb[:, t % 2, :], ALU.add).then_inc(s_z, 1)

            def variance(sources, start=True):
                for i, src in enumerate(sources):
                    if i == 0 and start:
                        ins = V.tensor_scalar(var_t, src, 1.0 / D, EPS, ALU.mult, ALU.add)
                    else:
                        me.wait()
                        ins = V.scalar_tensor_tensor(var_t, src, 1.0 / D, var_t, ALU.mult, ALU.add)
                    me.then(ins)
                me.wait()

            def rstd(k):
                dve.sem_inc(s_var, 1)
                dve.wait_ge(s_sqrt, k)
                me.then(V.reciprocal(rt, rt))
                me.wait()
                me.then(V.scalar_tensor_tensor(tmp_t, rt, -0.5, rt, ALU.mult, ALU.mult))
                me.wait()
                me.then(V.tensor_tensor(tmp_t, tmp_t, var_t, ALU.mult))
                me.wait()
                me.then(V.scalar_tensor_tensor(rt, tmp_t, 1.5, rt, ALU.add, ALU.mult))
                me.wait()

            def rt4():
                return rt.rearrange("p (o s) -> p o s", o=1).broadcast_to([P, 4, S])

            def h_group(l, g, n):
                buf = (bufA, bufB)[g % 2]
                me.then(V.scalar_tensor_tensor(ga[:, 4 * g:4 * g + 4], mod[:, 48 * l + KT + 4 * g:48 * l + KT + 4 * g + 4],
                                               1.0, prm[:, PRM_PRE + KT * l + 4 * g:PRM_PRE + KT * l + 4 * g + 4],
                                               ALU.add, ALU.mult))
                me.then(V.tensor_tensor(buf[:, :, :], xT[:, 4 * g:4 * g + 4, :], rt4(), ALU.mult))
                me.wait()
                for t in range(4):
                    k = 4 * g + t
                    ins = V.tensor_scalar(buf[:, t, :], buf[:, t, :], ga[:, k:k + 1],
                                          mod[:, 48 * l + k:48 * l + k + 1], ALU.mult, ALU.add)
                    me.then(ins)
                me.wait()
                dve.sem_inc(s_hf, 1)
                dve.wait_ge(s_yhi, n)
                V.tensor_tensor(H[:, 4 * g:4 * g + 4, S:2 * S], buf[:, :, :],
                                H[:, 4 * g:4 * g + 4, 0:S].bitcast(F32), ALU.subtract).then_inc(s_h, 1)

            V.memset(ones[:, :], 1.0).then_inc(s_tpc, 1)
            me.then(V.memset(cu[:, :, 0:2], 0.0))
            me.then(V.memset(ones_r[:, :].bitcast(F32), 1.0))
            dve.sem_inc(s_used, ADA_START * GROUPS)
            me.then(V.memset(c_cols[:, :, :], 0.0))
            me.wait()
            dve.sem_inc(s_tpc, 1)
            dve.sem_inc(s_z, 4)
            dve.sem_inc(s_yr, 4)
            for i, (col, n) in enumerate(((PRM_B, 96), (PRM_PRE, 112), (PRM_CW, 96))):
                dve.wait_ge(s_tp, i + 1)
                ins = V.tensor_copy(prm[:, col:col + n], Z[i][:, 0:n])
                if i < 2:
                    ins.then_inc(s_tpc, 1)
                else:
                    ins.then_inc(s_tpc, 1)
            dve.wait_ge(s_cs, 2)
            for k in range(ADA_START):
                g, part = k // 2, 1 - k % 2
                dve.wait_ge(s_adapart, GROUPS * (k + 1))
                V.tensor_copy(acc[:, :], Z[2 + k % 2][:, :]).then_inc(s_acc, 1)
                ada_low(k)
                mods(k, KT * part + 4 * g, 1)
                if k == 1:
                    dve.wait_ge(s_xsum, KT)
                    variance([SC[0][:, 0:S]])
                    rstd(1)
                if k == ADA_START - 1:
                    split(stage_pos(0, 0, 0) % SLOTS, 0, ck(0, 0, 0))
                if part == 0:
                    dve.wait_ge(s_mod, k + 1)
                    h_group(0, g, g + 1)

            for l in range(LAYERS):
                yhi0 = GROUPS + l * (TURNS + GROUPS + GROUPS)
                before = ada_before(l)
                span = CH_TURN + ADA_TURN[l] * GROUPS
                for w in range(1 if l == 0 else 2, LEAD):
                    split(stage_pos(l, 0, w) % SLOTS, w % 2, ck(l, 0, w))
                with dve.Fori(0, TURNS) as j:
                    me.loop(j, PER_TURN[l])
                    seen = 0
                    for w in range(LEAD, CH_TURN + LEAD):
                        for i in range(before[w]):
                            rel = stage_pos(l, 0, w) - before[w] + i
                            ada_chunk(rel % SLOTS, j * (16 * span // SLOTS) + 16 * (rel // SLOTS + 1), seen % GROUPS,
                                      seen % GROUPS == 0)
                            seen += 1
                            if seen % GROUPS == 0:
                                dve.sem_inc(s_acc, 1)
                                ada_low(ada_no(l, j, seen // GROUPS - 1))
                        split(stage_pos(l, 0, w) % SLOTS, w % 2, ck(l, j, w))
                        b, late = w // GROUPS - 1, w % GROUPS
                        if late == 0 and b != VV:
                            dst = {QK: bufA, GC: bufB, UU: bufA, GB: bufB, GG: bufA, GR: sg}[b]
                            if b == GB:
                                dve.wait_ge(s_cu, TURNS * l + 1 + j)
                            for t in range(TILES):
                                z_out_of(t, zlo_at(l, j, b) + t + 1, dst[:, t, :])
                        if (b, late) == (VV, 2):
                            for h in range(2):
                                dve.wait_ge(s_sc, 2 * TURNS * l + h + 1 + 2 * j)
                                if h == 0:
                                    dve.wait_ge(s_dec, 16 * (TURNS * l + 1) + 16 * j)
                                V.tensor_tensor(p_sb[:, h, 0:S], SC[h][:, 0:S], dec[:, h, :], ALU.mult)
                                V.tensor_tensor(p_sb[:, h, S:S + P], SC[h][:, S:S + P], dec[:, h, 0:P], ALU.mult)\
                                    .then_inc(s_p, 1)
                        if (b, late) == (GC, 2):
                            for h in range(2):
                                dve.wait_ge(s_in, 2 * TURNS * l + h + 1 + 2 * j)
                                for i in range(NT):
                                    me.then(V.bn_stats(stats[:, 2 * h + i, :], IN[h][:, i * DV:(i + 1) * DV]))
                            me.wait()
                            hold(dve, "dve")
                            for q in range(4):
                                ins = V.bn_aggr(mv[:, q, :], stats[:, q, :])
                            ins.then_inc(s_mv, 1)
                        if b == GR and late in (1, 2):
                            if late == 1:
                                dve.wait_ge(s_sgr, TURNS * l + 1 + j)
                                dve.wait_ge(s_tr, 2 * TURNS * l + 2 + 2 * j)
                            for q in (2 * late - 2, 2 * late - 1):
                                V.scalar_tensor_tensor(
                                    yr[:, bass.ds(j * 4 + q, 1), :].rearrange("p o s -> p (o s)"),
                                    SC[q // 2][:, (q % 2) * S:(q % 2 + 1) * S],
                                    prm[:, bass.ds(j * 4 + PRM_GN + KT * l + q, 1)], sg[:, q, :],
                                    ALU.mult, ALU.mult).then_inc(s_yr, 1)
                        for k in (k for k in range(CONV_K) if CONV_STEPS[k] == (b, late)):
                            if k == 0:
                                dve.wait_ge(s_cu, TURNS * l + 1 + j)
                                dve.wait_ge(s_tr, 2 * TURNS * l + 2 + 2 * j)
                            for t in range(TILES):
                                wk = prm[:, bass.ds(j * 4 + PRM_CW + 48 * l + KT * k + t, 1)]
                                if k == 0:
                                    ins = V.tensor_scalar(bufC[:, t, :], cu[:, t, 0:S], wk, None, ALU.mult)
                                else:
                                    ins = V.scalar_tensor_tensor(bufC[:, t, :], cu[:, t, k:k + S], wk,
                                                                 bufC[:, t, :], ALU.mult, ALU.add)
                                if k < CONV_K - 1:
                                    me.then(ins)
                            if k < CONV_K - 1:
                                me.wait()
                            else:
                                ins.then_inc(s_cv, 1)
                        if (b, late) == (GG, 1):
                            dve.wait_ge(s_sg, TURNS * l + 1 + j)
                            dve.wait_ge(s_cg, TURNS * l + 1 + j)
                            V.tensor_tensor(bufC[:, :, :], bufC[:, :, :], bufA[:, :, :], ALU.mult).then_inc(s_y, 1)
                        if (b, late) == (GG, 2):
                            dve.wait_ge(s_yhi, yhi0 + 1 + j)
                            V.tensor_tensor(Y2[:, bass.ds(j * 4, 4), S:2 * S], bufC[:, :, :],
                                            Y2[:, bass.ds(j * 4, 4), 0:S].bitcast(F32), ALU.subtract).then_inc(s_y2, 1)
                        if b in mod_points(l) and late == 1:
                            m = mod_points(l).index(b)
                            al, part = ADA_WHAT[l][m]
                            mods(ada_no(l, j, m), j * 4 + 48 * al + KT * part, b)
                    me.end(TURNS)

                def out_block(nb, first=False, last=False):
                    for w in range(LEAD if first else 1, OUT_CH + (0 if last and l == LAYERS - 1 else 1)):
                        split(w % SLOTS, w % 2, ck_out(l, nb, w))
                        if first and w < LEAD + GROUPS:
                            q = 4 * (w - LEAD)
                            dve.wait_ge(s_yhi, yhi0 + TURNS + w - LEAD + 1)
                            V.tensor_tensor(H[:, q:q + 4, S:2 * S], yr[:, q:q + 4, :],
                                            H[:, q:q + 4, 0:S].bitcast(F32), ALU.subtract).then_inc(s_hr, 1)
                        if last and w == OUT_CH - 2:
                            dve.wait_ge(s_osum, KT * l + 12)
                            variance([IN[0][:, 0:S], IN[0][:, S:2 * S], IN[1][:, 0:S]])
                    for t in range(TILES):
                        z_out_of(t, zlo_out(l, nb) + t + 1,
                                 yr[:, bass.ds(nb * 4 + t, 1), :].rearrange("p o s -> p (o s)"))

                dve.wait_ge(s_yr, 4 + 4 * TURNS * (l + 1))
                out_block(0, first=True)
                with dve.Fori(1, 3) as nb:
                    out_block(nb)
                out_block(3, last=True)
                dve.wait_ge(s_mod, ada_no(l, TURNS, 0))
                me.then(V.tensor_tensor(gp[:, :], mod[:, 48 * l + 2 * KT:48 * l + 3 * KT],
                                        prm[:, PRM_POST + KT * l:PRM_POST + KT * l + KT], ALU.mult))
                dve.wait_ge(s_osum, KT * (l + 1))
                variance([IN[1][:, S:2 * S]], start=False)
                rstd(2 * l + 2)
                for g in range(GROUPS):
                    me.then(V.tensor_tensor(yr[:, 4 * g:4 * g + 4, :], yr[:, 4 * g:4 * g + 4, :], rt4(), ALU.mult))
                    me.wait()
                    for t in range(4):
                        k = 4 * g + t
                        me.then(V.scalar_tensor_tensor(xT[:, k, :], yr[:, k, :], gp[:, k:k + 1], xT[:, k, :],
                                                       ALU.mult, ALU.add))
                    me.wait()
                    dve.sem_inc(s_xn, 1)
                if l < LAYERS - 1:
                    split(stage_pos(l + 1, 0, 1) % SLOTS, 1, ck(l + 1, 0, 1))
                    dve.wait_ge(s_xsum, KT * (l + 2))
                    variance([SC[0][:, 0:S]])
                    rstd(2 * l + 3)
                    for g in range(GROUPS):
                        h_group(l + 1, g, yhi0 + TURNS + GROUPS + g + 1)
            for g in range(GROUPS):
                dve.wait_ge(s_ot, 2 * g + 1)
                V.tensor_copy(stage[:, 0, g, :], (SC, IN)[g % 2][0][:, :]).then_inc(s_oc[0], 1)

        @block.gpsimd
        def _(pool):
            me = Steps(pool, s_pd)
            G = nc.gpsimd

            def step(ins):
                me.then(ins)
                me.wait()

            step(G.memset(mhalf[:, :], -0.5))
            ang, u, n = bufC[:, 1, :], bufC[:, 2, :], bufC[:, 3, :]
            pool.wait_ge(s_pos, 16)
            pool.wait_ge(s_par, 16 * 12)
            step(G.tensor_copy(u, bufC[:, 0, :].bitcast(I32)))
            step(G.tensor_scalar(ang, u, ident[:, P:P + 1], None, ALU.mult))
            turn = 2 * math.pi
            c1 = round(turn * 2 ** 9) / 2 ** 9
            c2 = round((turn - c1) * 2 ** 21) / 2 ** 21
            c3 = turn - c1 - c2
            whole = 1.5 * 2 ** 23
            for scale in (2.0 ** 20, 2.0 ** 10, 1.0):
                step(G.tensor_scalar(n, ang, 1.0 / (turn * scale), None, ALU.mult))
                step(G.tensor_scalar(n, n, whole, None, ALU.add))
                step(G.tensor_scalar(n, n, whole, None, ALU.subtract))
                for part in (c1, c2, c3):
                    step(G.tensor_scalar(u, n, part * scale, None, ALU.mult))
                    step(G.tensor_tensor(ang, ang, u, ALU.subtract))
            edge = float(np.nextafter(np.float32(math.pi), np.float32(0)))
            step(G.tensor_scalar(ang, ang, edge, None, ALU.min))
            step(G.tensor_scalar(ang, ang, -edge, None, ALU.max))
            pool.sem_inc(s_tab, 1)
            pool.wait_ge(s_sin, 2)
            step(G.tensor_tensor(cos_t[:, :], cos_t[:, :], cos_t[:, :], ALU.mult))
            step(G.tensor_scalar(cos_t[:, :], cos_t[:, :], -2.0, 1.0, ALU.mult, ALU.add))
            step(G.tensor_scalar(sin_t[:, :], sin_t[:, :], ident[:, P + 1:P + 2], None, ALU.mult))

            def all4(t):
                return t[:, :].rearrange("p (o s) -> p o s", o=1).broadcast_to([P, 4, S])

            for l in range(LAYERS):
                with pool.Fori(0, TURNS) as j:
                    me.loop(j, 5)
                    pool.wait_ge(s_z, z_at(l, j, VV))
                    me.then(G.tensor_tensor(bufC[:, :, :], bufA[:, :, :], all4(cos_t), ALU.mult))
                    pool.wait_ge(s_swap, 2 * TURNS * l + 2 + 2 * j)
                    me.then(G.tensor_tensor(bufB[:, :, :], bufB[:, :, :], all4(sin_t), ALU.mult))
                    me.wait()
                    G.tensor_tensor(bufC[:, :, :], bufC[:, :, :], bufB[:, :, :], ALU.add).then_inc(s_rope, 1)
                    pool.wait_ge(s_mv, TURNS * l + 1 + j)
                    hold(pool, "pool")
                    me.then(G.tensor_scalar(rs4[:, :], mv[:, :, 1], EPS, None, ALU.add))
                    me.wait()
                    me.then(G.tensor_tensor(rs4[:, :], rs4[:, :], mhalf[:, :], ALU.pow))
                    me.then(G.tensor_scalar(nb4[:, :], mv[:, :, 0], -1.0, None, ALU.mult))
                    me.wait()
                    G.tensor_tensor(nb4[:, :], nb4[:, :], rs4[:, :], ALU.mult).then_inc(s_rs, 1)
                    pool.wait_ge(s_z, z_at(l, j, GB))
                    G.tensor_tensor(cu[:, :, 2:S + 2], bufA[:, :, :], bufB[:, :, :], ALU.mult).then_inc(s_cu, 1)
                    pool.wait_ge(s_cv, TURNS * l + 1 + j)
                    G.tensor_tensor(bufC[:, :, :], bufC[:, :, :], bufB[:, :, :], ALU.mult).then_inc(s_cg, 1)
                    me.end(TURNS)

        @block.tensor
        def _(pe):
            T = nc.tensor
            I = ident[:, 0:P]

            def order(tiles, last):
                if last:
                    return [(t, a) for t in range(tiles) for a in range(CK)]
                return [(t, 2 * h + a) for h in range(2) for t in range(tiles) for a in range(2)]

            def chunk(parity, n, kc, rhs, z, nk=GROUPS, ready=None):
                for t, a in order(TILES, kc == nk - 1):
                    if kc == 0 and a == 0:
                        pe.wait_ge(s_z, z(t))
                    if t == 0 and a % 2 == 0:
                        pe.wait_ge(s_lo, 2 * n + a // 2 + 1)
                    wh = w_hi[:, 2 * parity + a // 2, a % 2, t * P:(t + 1) * P]
                    wl = w_lo[:, 2 * parity + a // 2, a % 2, t * P:(t + 1) * P]
                    act = rhs(CK * kc + a)
                    start = kc == 0 and a == 0
                    stop = kc == nk - 1 and a == CK - 1
                    if start:
                        T.matmul(Z[t][:, :], wh, act, start=True, stop=False)
                    ins = T.matmul(Z[t][:, 0:S], wl, act[:, 0:S], start=False, stop=False)
                    if not start:
                        ins = T.matmul(Z[t][:, :], wh, act, start=False, stop=stop)
                    if kc == nk - 1 and a == CK - 1:
                        ins.then_inc(s_pe, 1)
                    elif kc < nk - 1 and a % 2 and t == TILES - 1:
                        ins.then_inc(s_pe, 2)

            def v_chunk(parity, n, kc, z):
                for i, a in order(NT, kc == GROUPS - 1):
                    if kc == 0 and a == 0:
                        pe.wait_ge(s_z, z(i))
                    if i == 0 and a % 2 == 0:
                        pe.wait_ge(s_lo, 2 * n + a // 2 + 1)
                    wh = w_hi[:, 2 * parity + a // 2, a % 2, :]
                    wl = w_lo[:, 2 * parity + a // 2, a % 2, :]
                    hh = H[:, CK * kc + a, i * P:(i + 1) * P]
                    hl = H[:, CK * kc + a, S + i * P:S + (i + 1) * P]
                    T.matmul(Z[i][:, :], hh, wh, start=kc == 0 and a == 0, stop=False)
                    T.matmul(Z[i][:, :], hh, wl, start=False, stop=False)
                    ins = T.matmul(Z[i][:, :], hl, wh, start=False,
                                   stop=kc == GROUPS - 1 and a == CK - 1)
                    if kc == GROUPS - 1 and a == CK - 1:
                        ins.then_inc(s_pe, 2)
                    elif kc < GROUPS - 1 and a % 2 and i == NT - 1:
                        ins.then_inc(s_pe, 2)

            def ada_sum(k, b):
                pe.wait_ge(s_alo, k + 1)
                for t in range(TILES):
                    T.matmul(ada_bank(b)[:, 2 * t:2 * t + 2], acc_hi[:, t * P:(t + 1) * P], ones_r[:, :], start=True, stop=False)
                    ins = T.matmul(ada_bank(b)[:, 2 * t:2 * t + 2], acc_lo[:, t * P:(t + 1) * P], ones_r[:, :], start=False, stop=True)
                ins.then_inc(s_mm, 1)

            def x_sum(k):
                for g in range(GROUPS):
                    pe.wait_ge(s_xsq, GROUPS * k + g + 1)
                    for t in range(4):
                        T.matmul(SC[0][:, 0:S], ones[:, :], (bufA, bufB)[g % 2][:, t, :], start=g == 0 and t == 0,
                                 stop=g == 3 and t == 3).then_inc(s_xsum, 1)

            pe.wait_ge(s_par, 16 * 12)
            for i, n in enumerate((96, 112, 96)):
                T.transpose(Z[i][:, 0:n], bufA[0:n, i, 0:P], ident[0:n, 0:n]).then_inc(s_tp, 1)

            def x_transposes():
                pe.wait_ge(s_x, 32)
                rows = yr[:, :, :].rearrange("p t s -> p (t s)")
                for g in range(GROUPS):
                    if g >= 2:
                        pe.wait_ge(s_xc, 2 * (g - 1))
                    for i in range(2):
                        for q in range(2):
                            for tok in range(NT):
                                col = tok * D + (4 * g + 2 * i + q) * P
                                ins = T.transpose((SC, IN)[g % 2][i][:, q * S + tok * P:q * S + (tok + 1) * P],
                                                  rows[:, col:col + P], I)
                        ins.then_inc(s_tp, 1)

            pe.sem_inc(s_pe, 8)
            pe.wait_ge(s_tpc, 5)
            pe.wait_ge(s_cs, 2)
            for k in range(ADA_START):
                if k >= 2:
                    pe.wait_ge(s_acc, k - 1)
                for kc in range(GROUPS):
                    pe.wait_ge(s_stage[kc], 16 * (k + 1))
                    for a in range(CK):
                        ins = T.matmul(Z[2 + k % 2][COL * a:COL * (a + 1), :], c_cols[:, CK * kc + a, :], stage[:, kc, a, :],
                                       start=kc == 0, stop=kc == GROUPS - 1)
                    ins.then_inc(s_adapart, 1)
                if k == 0:
                    x_transposes()
                if k == 1:
                    x_sum(0)
                if k:
                    if k > 1:
                        pe.wait_ge(s_mod, k - 1)
                    ada_sum(k - 1, GR)
            pe.wait_ge(s_mod, ADA_START - 1)
            ada_sum(ADA_START - 1, GR)

            for l in range(LAYERS):
                with nc.Fori(0, TURNS, engines=(mybir.EngineType.PE,), hint_back_edge=True) as j:
                    for b in range(BLOCKS):
                        pb = b - 1 if b else GR
                        z0 = z_at(l, j, b) - (2 if pb == VV else 4)
                        for kc in range(GROUPS):
                            w = GROUPS * b + kc
                            if b == QK:
                                pe.wait_ge(s_h, GROUPS * l + kc + 1)
                            z = lambda t: z0 + min(t + 1, 2 if pb == VV else 4)
                            if b == VV:
                                v_chunk(w % 2, ck(l, j, w), kc, z)
                            else:
                                chunk(w % 2, ck(l, j, w), kc, lambda k: H[:, k, :], z)
                        if b == VV:
                            pe.wait_ge(s_rope, TURNS * l + 1 + j)
                            pe.wait_ge(s_yr, 4 * TURNS * l + 4 + 4 * j)
                            for h in range(2):
                                q, k = bufC[:, h, :], bufC[:, 2 + h, :]
                                T.matmul(SC[h][:, 0:S], k[:, 0:P], q, start=True, stop=True)
                                T.matmul(SC[h][:, S:S + P], k[:, P:S], q[:, P:S], start=True, stop=True).then_inc(s_sc, 1)
                        if b == GC:
                            for h in range(2):
                                pe.wait_ge(s_p, 2 * TURNS * l + h + 1 + 2 * j)
                                pe.wait_ge(s_z, z_at(l, j, GC))
                                v0, v1 = (v_sb[:, i, h * DV:(h + 1) * DV] for i in range(NT))
                                T.matmul(IN[h][:, 0:DV], p_sb[:, h, 0:P], v0, start=True, stop=True)
                                T.matmul(IN[h][:, DV:2 * DV], p_sb[:, h, P:2 * P], v0, start=True, stop=False)
                                T.matmul(IN[h][:, DV:2 * DV], p_sb[:, h, 2 * P:3 * P], v1, start=False, stop=True)\
                                    .then_inc(s_in, 1)
                        if b == UU:
                            pe.wait_ge(s_yn, TURNS * l + 1 + j)
                            for h in range(2):
                                for e in range(2):
                                    for i in range(NT):
                                        ins = T.transpose(SC[h][:, e * S + i * P:e * S + (i + 1) * P],
                                                          bufC[:, 2 * h + i, e * P:(e + 1) * P], I)
                                ins.then_inc(s_tr, 1)
                        if b in mod_points(l):
                            ada_sum(ada_no(l, j, mod_points(l).index(b)), b)

                def o_sum(nb):
                    pe.wait_ge(s_o, KT * l + 4 + 4 * nb)
                    for t in range(4):
                        dst = (IN[nb // 2][:, (nb % 2) * S:(nb % 2 + 1) * S])
                        T.matmul(dst, ones[:, :], bufA[:, t, :], start=t == 0, stop=t == 3).then_inc(s_osum, 1)

                def src(k):
                    return Y2[:, k, :] if k < KT else H[:, k - KT, :]

                for nb in range(D // BLK):
                    for w in range(OUT_CH):
                        if nb == 0:
                            if w < GROUPS:
                                pe.wait_ge(s_y2, TURNS * l + w + 1)
                            else:
                                pe.wait_ge(s_hr, GROUPS * l + w - GROUPS + 1)
                        chunk(w % 2, ck_out(l, nb, w), w, src, lambda t: z_out(l, nb) - 4 + t + 1, nk=OUT_CH)
                        if w == 1 and nb:
                            if nb == 1:
                                pe.wait_ge(s_mod, ada_no(l, TURNS, 0))
                            o_sum(nb - 1)
                o_sum(D // BLK - 1)
                if l < LAYERS - 1:
                    x_sum(l + 1)
            for g in range(GROUPS):
                pe.wait_ge(s_xn, GROUPS * LAYERS + g + 1)
                if g >= 2:
                    pe.wait_ge(s_oc[0], g - 1)
                    pe.wait_ge(s_oc[1], g - 1)
                for i in range(NT):
                    for t in range(4):
                        ins = T.transpose((SC, IN)[g % 2][i][:, t * P:(t + 1) * P],
                                          xT[:, 4 * g + t, i * P:(i + 1) * P], I)
                    ins.then_inc(s_ot, 1)


PER_TURN = [ADA_TURN[l] * GROUPS * CK + 4 + (CONV_K - 1) * TILES for l in range(LAYERS)]


CONV_STEPS = ((UU, 2), (GB, 0), (GB, 2))


def constants():
    half = DK // 2
    f = (np.float32(10000.0) ** (-np.arange(half, dtype=np.float32) / np.float32(half))).astype(np.float32)
    cst = np.zeros((P, P + 2), np.float32)
    cst[:, :P] = np.eye(P, dtype=np.float32)
    cst[:, P] = np.concatenate([f, f])
    cst[:, P + 1] = np.concatenate([-np.ones(half), np.ones(half)])
    gamma = 1.0 - 2.0 ** (-5.0 - np.arange(HEADS))
    diff = np.arange(S)[None, :] - np.arange(P)[:, None]
    dec = np.where(diff[None] >= 0, gamma[:, None, None] ** np.maximum(diff, 0)[None], 0.0) * DK ** -0.5
    dec = dec.reshape(TURNS, 2, P, S).transpose(0, 2, 1, 3)
    dec = np.concatenate([dec, dec[:1]])
    return cst, np.ascontiguousarray(dec.astype(np.float32))


_INS = ["x", "c", "positions", "norm_pre", "norm_post", "w_ada", "b_ada", "w_in", "conv_w", "gn_gain", "w_out"]


def kernel(**inputs):
    import concourse.bacc as bacc
    from concourse.bass_utils import run_bass_kernel_spmd

    nc = bacc.Bacc("TRN2", target_bir_lowering=False, num_devices=1)
    arrays, args = {}, []
    for name in _INS:
        a = np.ascontiguousarray(inputs[name])
        arrays[f"in_{name}"] = a
        args.append(nc.dram_tensor(f"in_{name}", a.shape, mybir.dt.from_np(a.dtype), kind="ExternalInput").ap())
    for name, a in zip(("consts", "decay"), constants()):
        arrays[name] = a
        args.append(nc.dram_tensor(name, a.shape, F32, kind="ExternalInput").ap())
    args.append(nc.dram_tensor("out", (1, S, D), F32, kind="ExternalOutput").ap())
    build(nc, *args)
    r = run_bass_kernel_spmd(nc, [arrays], core_ids=[0])
    return r.results[0]["out"]
```

```python
import math
from contextlib import ExitStack

import numpy as np

import concourse.bass as bass
from concourse import mybir

F32 = mybir.dt.float32
F32R = mybir.dt.float32r
I32 = mybir.dt.int32
ALU = mybir.AluOpType
ACT = mybir.ActivationFunctionType

P = 128
D = 2048
S = 256
LAYERS = 2
KT = D // P
NT = S // P
W_CONV = 2048
HEADS = 8
DK, DV = 128, 256
W_QK = HEADS * DK
CONV_K = 3
EPS = 1e-6
COL_GB, COL_GC, COL_U, COL_G = 0, W_CONV, 2 * W_CONV, 3 * W_CONV
COL_Q = 4 * W_CONV
COL_V = COL_Q + 2 * W_QK
COL_GR = COL_V + HEADS * DV
BLK = 512
TILES = BLK // P
CK = 4
GROUPS = KT // CK
SLOTS = 4
QK, VV, GC, UU, GB, GG, GR = range(7)
BLOCKS = 7
TURNS = 4
CH_TURN = BLOCKS * GROUPS
CH_OUT = (2 * D // (CK * P)) * (D // BLK)
OUT_CH = 2 * D // (CK * P)
CH_LAYER = TURNS * CH_TURN + CH_OUT
POOL_G = 3
GROUP_ORDER = (0, 1, 3, 2)
FIRST_AT = (((5, 0), (5, 1), (5, 2), (5, 3)),
            ((6, 0), (6, 1), (6, 2), (6, 3)),
            ((7, 0), (8, 0), (8, 1), (8, 1)))
SUM_AT = 1
CLOCK_X, CLOCK_SUMS, CLOCK_H = 10, 6, 12
GATE_AT = 3
LEAD = 4
ADA_FRONT = 3
CONV_STEPS = ((UU, 2), (GB, 0), (GB, 2))
COL = 32
ADA_START = 8
ADA_TURN = (3, 1)
Z_TURN = 26
Z_OUT = D // P
Z_LAYER = TURNS * Z_TURN + Z_OUT
LO_TURN = 24
LO_LAYER = TURNS * LO_TURN + Z_OUT
PER_TURN = [ADA_TURN[l] * GROUPS * CK + 4 + (CONV_K - 1) * TILES for l in range(LAYERS)]
PRM_B, PRM_PRE, PRM_POST, PRM_GN, PRM_C, PRM_CW = 0, 96, 128, 160, 192, 208
PRM = 304


def ada_before(layer):
    n = ADA_TURN[layer] * GROUPS
    at = [0] * (CH_TURN + LEAD)
    for i in range(n):
        at[LEAD + 1 + (i * (CH_TURN - LEAD)) // n] += 1
    return at


def mod_points(layer):
    return (GC, GB, GR) if layer == 0 else (GR,)


def build(nc, x, c, positions, norm_pre, norm_post, w_ada, b_ada, w_in, conv_w, gn_gain, w_out,
          consts, decay, out):
    ctx = ExitStack()
    with ctx:
        def sb(name, shape, dt=F32):
            return ctx.enter_context(nc.sbuf_tensor(name, shape, dt))

        def sem(name):
            return ctx.enter_context(nc.semaphore(name))

        xT = sb("xT", [P, KT, S])
        H = sb("H", [P, KT, 2 * S], F32R)
        Y2 = sb("Y2", [P, KT, 2 * S], F32R)
        yr = sb("yr", [P, KT, S])
        stage = sb("stage", [P, SLOTS, CK, BLK])
        w_hi = sb("w_hi", [P, 4, 2, BLK], F32R)
        w_lo = sb("w_lo", [P, 4, 2, BLK], F32R)
        bufA = sb("bufA", [P, 4, S])
        bufB = sb("bufB", [P, 4, S])
        bufC = sb("bufC", [P, 4, S])
        cu = sb("cu", [P, 4, S + 2])
        v_sb = sb("v_sb", [P, NT, 2 * DV])
        sg = sb("sg", [P, 4, S])
        p_sb = sb("p_sb", [P, 2, 3 * P])
        lo_sb = sb("lo_sb", [P, 2, S])
        dec = sb("dec", [P, 2, S])
        cos_t = sb("cos_t", [P, S])
        sin_t = sb("sin_t", [P, S])
        acc = sb("acc", [P, BLK])
        acc_hi = sb("acc_hi", [P, BLK], F32R)
        acc_lo = sb("acc_lo", [P, BLK], F32R)
        ident = sb("ident", [P, P + 2])
        ones = sb("ones", [P, P])
        ones_r = sb("ones_r", [P, 2], F32R)
        prm = sb("prm", [P, PRM])
        mod = sb("mod", [P, LAYERS * 3 * KT])
        c_silu = sb("c_silu", [P, KT])
        c_cols = sb("c_cols", [P, KT, COL])
        ga = sb("ga", [P, KT])
        gp = sb("gp", [P, KT])
        stats = sb("stats", [P, 4, 6])
        mv = sb("mv", [P, 4, 2])
        rs4 = sb("rs4", [P, 4])
        nb4 = sb("nb4", [P, 4])
        var2 = sb("var2", [P, NT])
        rs2 = sb("rs2", [P, NT])
        mhalf = sb("mhalf", [P, 4])
        diag, rt_sb = (cu[:, t, 2:S + 2] for t in range(2))

        Z = [ctx.enter_context(nc.psum_tensor(f"Z{t}", [P, 2 * S], F32)) for t in range(4)]
        SC = [ctx.enter_context(nc.psum_tensor(f"SC{t}", [P, 2 * S], F32)) for t in range(2)]
        IN = [ctx.enter_context(nc.psum_tensor(f"IN{t}", [P, 2 * S], F32)) for t in range(2)]

        s_par = sem("params_loaded")
        s_x = sem("x_loaded")
        s_pos = sem("positions_loaded")
        s_dec = sem("decay_loaded")
        s_stage = [sem(f"stage_loaded{i}") for i in range(SLOTS)]
        s_k = [sem(f"k_columns_loaded{i}") for i in range(GROUPS)]
        s_used = sem("stage_used")
        s_hi = sem("hi_done")
        s_lo = sem("lo_done")
        s_pe = sem("pe_tiles")
        s_zlo = sem("z_lo_copied")
        s_z = sem("z_free")
        s_swap = sem("qk_swapped")
        s_rope = sem("rope_done")
        s_sgr = sem("silu_gr_done")
        s_sc = sem("scores_done")
        s_p = sem("p_done")
        s_in = sem("inner_done")
        s_mv = sem("head_stats_done")
        s_rs = sem("head_rstd_done")
        s_yn = sem("heads_normalised")
        s_tr = sem("heads_transposed")
        s_yr = sem("yret_done")
        s_cu = sem("cu_done")
        s_cv = sem("conv_done")
        s_cg = sem("conv_gated")
        s_sg = sem("silu_g_done")
        s_y = sem("yconv_done")
        s_yhi = sem("y_hi_done")
        s_y2 = sem("yconv_split")
        s_hr = sem("yret_split")
        s_acc = sem("ada_acc_done")
        s_ahi = sem("ada_hi_done")
        s_alo = sem("ada_lo_done")
        s_mm = sem("ada_summed")
        s_mod = sem("mod_done")
        s_o = sem("o_squared")
        s_gp = sem("gate_gain_done")
        s_ou = sem("o_gated")
        s_opre = sem("o_squares_added")
        s_osum = sem("o_summed")
        s_xn = sem("x_new")
        s_xp = sem("x_new_last_group")
        s_rt2 = sem("o_rstd_spread_again")
        s_rtsb = sem("o_rstd_copied")
        s_xsq = sem("x_squared")
        s_xsum = sem("x_summed")
        s_var = sem("variance_done")
        s_adapart = sem("ada_chunk_multiplied")
        s_pow = sem("rstd_done")
        s_diag = sem("rstd_on_diagonals")
        s_rt = sem("rstd_spread")
        s_hf = sem("h_scaled")
        s_hhi = sem("h_hi_done")
        s_h = sem("h_split")
        s_tp = sem("start_transposes")
        s_tpc = sem("start_copied")
        s_cs = sem("c_silu_done")
        s_tab = sem("angle_done")
        s_xc = sem("x_copied")
        s_sin = sem("sines_done")
        s_ot = sem("out_transposed")
        s_oc = sem("out_copied")
        s_ocv = sem("out_copied_last")
        s_out = sem("out_stored")
        s_vd = sem("vector_step")
        s_pd = sem("pool_step")

        s_held = {e: sem(f"{e}_held") for e in ("sp", "dve", "pool")}

        block = ctx.enter_context(nc.Block())

        def hold(eng, name):
            eng.sem_inc(s_held[name], 1)

        class Steps:

            def __init__(self, eng, s):
                self.eng, self.s, self.n, self.turn, self.per = eng, s, 0, None, 0

            def then(self, ins):
                ins.then_inc(self.s, 1)
                self.n += 1
                self.last = self.n if self.turn is None else self.n + self.turn * self.per

            def wait(self):
                self.eng.wait_ge(self.s, self.last)

            def loop(self, turn, per):
                self.turn, self.per, self.at = turn, per, self.n

            def end(self, turns):
                assert self.n - self.at == self.per, (self.n - self.at, self.per)
                self.n += self.per * (turns - 1)
                self.turn = None

        def stage_pos(layer, j, w):
            base = ADA_START * GROUPS
            for earlier in range(layer):
                base += TURNS * (CH_TURN + ADA_TURN[earlier] * GROUPS) + CH_OUT
            return base + w + sum(ada_before(layer)[:w + 1]) + j * (CH_TURN + ADA_TURN[layer] * GROUPS)

        def start_pos(w):
            return GROUPS * (ADA_START - LEAD + 1) + w * (GROUPS + 1)

        def start_ada_pos(k, kc):
            return GROUPS * k + kc + max(0, k - (ADA_START - LEAD))

        def out_pos(layer, nb, w):
            return stage_pos(layer, TURNS, 0) + OUT_CH * nb + w

        def ck(layer, j, w):
            return CH_LAYER * layer + w + j * CH_TURN

        def ck_out(layer, nb, w):
            return CH_LAYER * layer + TURNS * CH_TURN + w + nb * OUT_CH

        def z_at(layer, j, b):
            return 4 + Z_LAYER * layer + 4 * b - (2 if b > VV else 0) + j * Z_TURN

        def zlo_at(layer, j, b):
            return LO_LAYER * layer + 4 * b - (4 if b > VV else 0) + j * LO_TURN

        def z_out(layer, nb):
            return 4 + Z_LAYER * layer + TURNS * Z_TURN + nb * 4

        def zlo_out(layer, nb):
            return LO_LAYER * layer + TURNS * LO_TURN + nb * 4

        def ada_no(layer, j, m):
            return ADA_START + (TURNS * ADA_TURN[0] if layer else 0) + m + j * ADA_TURN[layer]

        def row_bank(k):
            return Z[2 + k] if k < 2 else (IN[0], SC[1])[k % 2]

        def ada_bank(b):
            return SC[1] if b == GC else IN[1]

        def out_bank(n, i):
            return (Z[0:2], Z[2:4], SC, Z[0:2])[n][i]

        ADA_WHAT = (((0, 2), (1, 1), (1, 0)), ((1, 2),))

        @block.sync
        def _(sp):
            def load(slot, pos, dst, src, first=False):
                if not first:
                    sp.wait_ge(s_used, pos - SLOTS + 1)
                    hold(sp, "sp")
                sp.dma_start(dst, src).then_inc(s_stage[slot], 16)

            def rows(w, kc):
                return w[kc * CK * P:(kc + 1) * CK * P, :].rearrange("(a p) n -> p a n", p=P)

            pr = yr[:, :, :].rearrange("p t s -> p (t s)")
            small = [(ident[:, :], consts), (bufA[96:112, 1, 0:P], c[0, :].rearrange("(r q) -> r q", q=P))]
            for l in range(LAYERS):
                small.append((bufA[48 * l:48 * l + 48, 0, 0:P], b_ada[l, :].rearrange("(r q) -> r q", q=P)))
                for i, g in enumerate((norm_pre, norm_post, gn_gain)):
                    r = 32 * i + 16 * l
                    small.append((bufA[r:r + 16, 1, 0:P], g[l, :].rearrange("(r q) -> r q", q=P)))
                small.append((bufA[48 * l:48 * l + 48, 2, 0:P],
                              conv_w[l, :, :].rearrange("k (r q) -> (k r) q", q=P)))

            def load_qk(l, j, kc, slot):
                dst, src = stage[:, slot, :, :], rows(w_in[l, :, :], kc)
                sp.dma_start(dst[:, :, 0:2 * DK], src[:, :, bass.ds(j * 2 * DK + COL_Q, 2 * DK)])\
                    .then_inc(s_stage[slot], 16)
                sp.dma_start(dst[:, :, 2 * DK:], src[:, :, bass.ds(j * 2 * DK + COL_Q + W_QK, 2 * DK)])\
                    .then_inc(s_k[kc], 16)

            pos = 0
            for k in range(ADA_START):
                g, part = k // 2, 1 - k % 2
                for kc in range(GROUPS + (1 if k >= ADA_START - LEAD else 0)):
                    first_w = k - (ADA_START - LEAD)
                    if pos >= SLOTS:
                        if pos - SLOTS in [start_pos(w) for w in range(LEAD)]:
                            sp.wait_ge(s_used, GROUPS * ADA_START + first_w)
                        else:
                            old = pos - SLOTS - sum(start_pos(w) < pos - SLOTS for w in range(LEAD))
                            sp.wait_ge(s_adapart, old + 1)
                    if kc == GROUPS:
                        assert pos == start_pos(first_w)
                        load_qk(0, 0, first_w, pos % SLOTS)
                    else:
                        assert pos == start_ada_pos(k, kc)
                        col = part * D + g * BLK
                        load(pos % SLOTS, pos, stage[:, pos % SLOTS, :, :],
                             rows(w_ada[0, :, :], kc)[:, :, col:col + BLK], first=True)
                    if pos < 2:
                        for dst, src in small[pos * len(small) // 2:(pos + 1) * len(small) // 2]:
                            sp.dma_start(dst, src).then_inc(s_par, 16)
                    if pos == SLOTS - 1:
                        for i in range(NT):
                            sp.dma_start(pr[:, i * D:(i + 1) * D], x[0, i * P:(i + 1) * P, :]).then_inc(s_x, 16)
                    pos += 1
            sp.wait_ge(s_adapart, GROUPS * ADA_START)
            sp.dma_start(dec[:, :, :], decay[0, :, :, :]).then_inc(s_dec, 16)

            def turn(l, j, first=0):
                before = ada_before(l)
                ada = 0
                for w in range(first, CH_TURN):
                    for i in range(before[w]):
                        al, part = ADA_WHAT[l][ada // GROUPS]
                        rel = stage_pos(l, 0, w) - before[w] + i
                        p = stage_pos(l, j, w) - before[w] + i
                        load(rel % SLOTS, p, stage[:, rel % SLOTS, :, :],
                             rows(w_ada[al, :, :], ada % GROUPS)[:, :, bass.ds(j * BLK + part * D, BLK)])
                        ada += 1
                    slot, p = stage_pos(l, 0, w) % SLOTS, stage_pos(l, j, w)
                    b, kc = divmod(w, GROUPS)
                    if b == QK:
                        sp.wait_ge(s_used, p - SLOTS + 1)
                        hold(sp, "sp")
                        load_qk(l, j, kc, slot)
                    else:
                        col = {VV: COL_V, GR: COL_GR, GC: COL_GC, UU: COL_U, GB: COL_GB, GG: COL_G}[b]
                        load(slot, p, stage[:, slot, :, :],
                             rows(w_in[l, :, :], kc)[:, :, bass.ds(j * BLK + col, BLK)])
                    if w == CH_TURN - 4:
                        sp.wait_ge(s_p, 2 * TURNS * l + 2 + 2 * j)
                        hold(sp, "sp")
                        sp.dma_start(dec[:, :, :], decay[bass.ds(j + 1, 1), :, :, :]
                                     .rearrange("o p h s -> p (o h) s")).then_inc(s_dec, 16)

            for l in range(LAYERS):
                if l == 0:
                    turn(0, 0, first=LEAD)
                with sp.Fori(1 if l == 0 else 0, TURNS) as j:
                    turn(l, j)
                for kc in range(GROUPS):
                    sp.sem_inc(s_k[kc], 16)
                with sp.Fori(0, D // BLK) as nb:
                    for w in range(OUT_CH):
                        load(w % SLOTS, out_pos(l, nb, w), stage[:, w % SLOTS, :, :],
                             rows(w_out[l, :, :], w)[:, :, bass.ds(nb * BLK, BLK)])
            for n, g in enumerate(GROUP_ORDER):
                for i in (range(NT) if n < GROUPS - 1 else (1, 0)):
                    if (n, i) == (GROUPS - 1, 0):
                        sp.wait_ge(s_ocv, 1)
                    else:
                        sp.wait_ge(s_oc, NT * n + min(i, GROUPS - 1 - n) + 1)
                    sp.dma_start(out[0, i * P:(i + 1) * P, g * BLK:(g + 1) * BLK],
                                 stage[:, i, g, :]).then_inc(s_out, 16)
            sp.wait_ge(s_out, 16 * GROUPS * NT)

        @block.scalar
        def _(act):
            def split(slot, value, w, n, block=GROUPS):
                parity = w % 2
                act.wait_ge(s_stage[slot], value)
                for h in range(2):
                    act.wait_ge(s_pe, 4 * n + (4 if h or w % block == 1 else 2))
                    nc.scalar.copy(w_hi[:, 2 * parity + h, :, :],
                                   stage[:, slot, 2 * h:2 * h + 2, :]).then_inc(s_hi, 1)

            def z_low(pe, t, zlo, z):
                act.wait_ge(s_pe, pe)
                act.wait_ge(s_z, z)
                nc.scalar.copy(lo_sb[:, t % 2, :], Z[t][:, S:2 * S]).then_inc(s_zlo, 1)

            def ada_hi(k, first=False):
                act.wait_ge(s_acc, k + 1)
                if not first:
                    act.wait_ge(s_mm, k)
                nc.scalar.copy(acc_hi[:, :], acc[:, :]).then_inc(s_ahi, 1)

            def x_squares(base, k):
                for i, g in enumerate(GROUP_ORDER):
                    for half in range(2):
                        if k and g == POOL_G:
                            act.wait_ge(s_xp, k)
                        else:
                            act.wait_ge(s_xn, base + 2 * g + half + 1)
                        if i >= 2:
                            act.wait_ge(s_xsum, KT * k + 4 * (i - 2) + 2 * half + 2)
                        nc.scalar.activation((bufA, bufB)[i % 2][:, 2 * half:2 * half + 2, :],
                                             xT[:, 4 * g + 2 * half:4 * g + 2 * half + 2, :],
                                             ACT.Square).then_inc(s_xsq, 1)

            def h_hi(l, g):
                if l == 0:
                    act.wait_ge(s_mod, 2 * g + 2)
                for t in range(4):
                    k = 4 * g + t
                    act.wait_ge(s_hf, KT * l + k + 1)
                    nc.scalar.activation(H[:, k, 0:S], (bufA, bufB)[g % 2][:, t, :], ACT.Identity,
                                         bias=mod[:, 48 * l + k:48 * l + k + 1]).then_inc(s_hhi, 1)

            act.dma_start(bufC[:, 0, :].bitcast(I32),
                          positions.rearrange("a s -> (a s)").partition_broadcast(P)).then_inc(s_pos, 16)
            act.wait_ge(s_tpc, 4)
            nc.scalar.activation(c_cols[:, :, 0], prm[:, PRM_C:PRM_C + KT], ACT.Silu).then_inc(s_cs, 1)
            nc.scalar.activation(c_silu[:, :], prm[:, PRM_C:PRM_C + KT], ACT.Silu).then_inc(s_cs, 1)
            for g in range(GROUPS):
                for i in range(2):
                    act.wait_ge(s_tp, 3 + 2 * g + i + 1)
                    nc.scalar.copy(xT[:, 4 * g + 2 * i:4 * g + 2 * i + 2, :],
                                   (SC, IN)[g % 2][i][:, :].rearrange("p (t s) -> p t s", t=2)).then_inc(s_xc, 1)
            act.wait_ge(s_xc, 2 * GROUPS)
            act.sem_inc(s_xn, 2 * GROUPS)
            def first_split(l, w):
                p = stage_pos(l, 0, w) if l else start_pos(w)
                act.wait_ge(s_k[w], 16 * ((TURNS + 1) * l + 1))
                split(p % SLOTS, 16 * (p // SLOTS + 1), w, ck(l, 0, w))

            x_squares(0, 0)
            ada_hi(0, first=True)
            ada_hi(1)
            h_hi(0, 0)
            act.wait_ge(s_tab, 1)
            nc.scalar.activation(sin_t[:, :], bufC[:, 1, :], ACT.Sin).then_inc(s_sin, 1)
            nc.scalar.activation(cos_t[:, :], bufC[:, 1, :], ACT.Sin, scale=0.5).then_inc(s_sin, 1)
            for k in range(2, ADA_START):
                ada_hi(k)
                if ADA_START - LEAD <= k:
                    first_split(0, k - (ADA_START - LEAD))
                if k % 2:
                    h_hi(0, k // 2)

            for l in range(LAYERS):
                before = ada_before(l)
                span = CH_TURN + ADA_TURN[l] * GROUPS
                if l:
                    for g in range(GROUPS):
                        h_hi(l, g)
                for w in range(LEAD if l == 0 else 2, LEAD):
                    first_split(l, w)
                with act.Fori(0, TURNS) as j:
                    seen = 0
                    for w in range(LEAD, CH_TURN + LEAD):
                        rel = stage_pos(l, 0, w)
                        if w >= CH_TURN:
                            act.wait_ge(s_k[w - CH_TURN], j * 16 + 16 * ((TURNS + 1) * l + 2))
                        split(rel % SLOTS, j * (16 * span // SLOTS) + 16 * (rel // SLOTS + 1), w, ck(l, j, w))
                        seen += before[w]
                        if before[w] and seen % GROUPS == 0:
                            ada_hi(ada_no(l, j, seen // GROUPS - 1))
                        b = w // GROUPS - 1
                        if (b, w % GROUPS) == (GC, 3):
                            act.wait_ge(s_rs, TURNS * l + 1 + j)
                            for q in range(4):
                                ins = nc.scalar.activation(bufC[:, q, :], IN[q // 2][:, (q % 2) * DV:(q % 2 + 1) * DV],
                                                           ACT.Identity, bias=nb4[:, q:q + 1], scale=rs4[:, q:q + 1])
                            ins.then_inc(s_yn, 1)
                        if (b, w % GROUPS) == (GG, 3):
                            act.wait_ge(s_y, TURNS * l + 1 + j)
                            nc.scalar.copy(Y2[:, bass.ds(j * 4, 4), 0:S], bufC[:, :, :]).then_inc(s_yhi, 1)
                        if w % GROUPS:
                            continue
                        if b == VV:
                            for i in range(NT):
                                act.wait_ge(s_pe, 8 + 4 * ck(l, j, w - 1) + 2 * i + 2)
                                nc.scalar.copy(v_sb[:, i, :], Z[i][:, :]).then_inc(s_z, 1)
                        else:
                            for t in range(TILES):
                                z_low(8 + 4 * ck(l, j, w - 1) + t + 1, t, zlo_at(l, j, b), z_at(l, j, b) + max(0, t - 1))
                        if b == QK:
                            act.wait_ge(s_z, z_at(l, j, b + 1))
                            nc.scalar.copy(bufB[64:128, :, :], bufA[0:64, :, :]).then_inc(s_swap, 1)
                            nc.scalar.copy(bufB[0:64, :, :], bufA[64:128, :, :]).then_inc(s_swap, 1)
                        if b == GR:
                            act.wait_ge(s_z, z_at(l, j, b + 1))
                            nc.scalar.activation(sg[:, :, :], sg[:, :, :], ACT.Silu).then_inc(s_sgr, 1)
                        if b == GG:
                            act.wait_ge(s_z, z_at(l, j, b + 1))
                            nc.scalar.activation(bufA[:, :, :], bufA[:, :, :], ACT.Silu).then_inc(s_sg, 1)

                def out_block(nb, first=False, last=False):
                    for w in range(LEAD if first else 1, OUT_CH + (0 if last else 1)):
                        pos = out_pos(l, 0, w)
                        split(w % SLOTS, nb * (16 * OUT_CH // SLOTS) + 16 * (pos // SLOTS + 1), w,
                              ck_out(l, nb, w), OUT_CH)
                        if first and w < LEAD + GROUPS:
                            if w == LEAD:
                                act.wait_ge(s_pe, 8 + 4 * ck_out(l, 0, 0))
                                act.wait_ge(s_yr, 4 + 4 * TURNS * (l + 1))
                            q = 4 * (w - LEAD)
                            nc.scalar.copy(H[:, q:q + 4, 0:S], yr[:, q:q + 4, :]).then_inc(s_yhi, 1)
                        if not first and w == GATE_AT:
                            gate(nb - 1)
                    if not last:
                        out_z(nb, first)

                def out_z(nb, first=False):
                    def square(t):
                        act.wait_ge(s_z, z_out(l, nb) + t + 1)
                        nc.scalar.activation(bufA[:, t, :], yr[:, bass.ds(nb * 4 + t, 1), :].rearrange("p o s -> p (o s)"),
                                             ACT.Square).then_inc(s_o, 1)

                    for t in range(TILES):
                        z_low(8 + 4 * ck_out(l, nb, OUT_CH - 1) + t + 1, t, 0, z_out(l, nb) + max(0, t - 1))
                        if t == 0 and not first:
                            act.wait_ge(s_opre, (D // BLK - 1) * l + nb)
                        if t:
                            square(t - 1)
                    square(TILES - 1)

                def gate(nb):
                    act.wait_ge(s_gp, l + 1)
                    act.wait_ge(s_o, KT * l + nb * 4 + 4)
                    for t in range(TILES):
                        o = yr[:, bass.ds(nb * 4 + t, 1), :].rearrange("p o s -> p (o s)")
                        nc.scalar.activation(o, o, ACT.Copy, scale=gp[:, bass.ds(nb * 4 + t, 1)]).then_inc(s_ou, 1)

                out_block(0, first=True)
                with act.Fori(1, 3) as nb:
                    out_block(nb)
                out_block(3, last=True)
                if l < LAYERS - 1:
                    first_split(l + 1, 0)
                    out_z(3)
                    gate(3)
                    first_split(l + 1, 1)
                else:
                    out_z(3)
                    gate(3)
                act.wait_ge(s_rt2, l + 1)
                nc.scalar.copy(rt_sb, IN[1][:, S:2 * S]).then_inc(s_rtsb, 1)
                if l < LAYERS - 1:
                    x_squares(2 * GROUPS + 2 * POOL_G * l, l + 1)
            for n, g in enumerate(GROUP_ORDER):
                for i in (range(NT) if n < GROUPS - 1 else (1,)):
                    act.wait_ge(s_ot, NT * n + i + 1)
                    nc.scalar.copy(stage[:, i, g, :], out_bank(n, i)[:, :]).then_inc(s_oc, 1)

        @block.vector
        def _(dve):
            me = Steps(dve, s_vd)
            V = nc.vector

            def low(slot, parity, n):
                for h in range(2):
                    dve.wait_ge(s_hi, 2 * n + h + 1)
                    V.tensor_tensor(w_lo[:, 2 * parity + h, :, :], stage[:, slot, 2 * h:2 * h + 2, :],
                                    w_hi[:, 2 * parity + h, :, :].bitcast(F32), ALU.subtract).then_inc(s_lo, 1)

            def used(n, count=1):
                dve.wait_ge(s_lo, 2 * n + 2)
                dve.sem_inc(s_used, count)

            def split(slot, parity, n):
                low(slot, parity, n)
                used(n)

            def ada_chunk(slot, kc, part):
                for a in part:
                    k = CK * kc + a
                    w = stage[:, slot, a, :]
                    if k == 0:
                        ins = V.tensor_scalar(acc[:, :], w, c_silu[:, k:k + 1], None, ALU.mult)
                    else:
                        me.wait()
                        ins = V.scalar_tensor_tensor(acc[:, :], w, c_silu[:, k:k + 1], acc[:, :],
                                                     ALU.mult, ALU.add)
                    me.then(ins)
                me.wait()

            def ada_low(k):
                dve.wait_ge(s_ahi, k + 1)
                V.tensor_tensor(acc_lo[:, :], acc[:, :], acc_hi[:, :].bitcast(F32), ALU.subtract).then_inc(s_alo, 1)

            def mods(k, col, bank):
                dve.wait_ge(s_mm, k + 1)
                V.tensor_tensor(mod[:, bass.ds(col, 4)], ada_bank(bank)[:, 0:8:2], prm[:, bass.ds(col, 4)], ALU.add)\
                    .then_inc(s_mod, 1)

            def z_out_of(t, zlo, dst):
                dve.wait_ge(s_zlo, zlo)
                V.tensor_tensor(dst, Z[t][:, 0:S], lo_sb[:, t % 2, :], ALU.add).then_inc(s_z, 1)

            def rstd(k, bank):
                by_token = diag.rearrange("p (i q) -> p i q", i=NT)
                every = ident[:, 0:P].rearrange("p (o q) -> p o q", o=1).broadcast_to([P, NT, P])
                me.then(V.tensor_tensor(by_token, bank[:, 0:S].rearrange("p (i q) -> p i q", i=NT), every, ALU.mult))
                me.wait()
                me.then(V.tensor_reduce(var2[:, :], by_token, mybir.AxisListType.X, ALU.add))
                me.wait()
                me.then(V.tensor_scalar(var2[:, :], var2[:, :], 1.0 / D, EPS, ALU.mult, ALU.add))
                me.wait()
                dve.sem_inc(s_var, 1)
                dve.wait_ge(s_pow, k)
                for i in range(NT):
                    ins = V.tensor_scalar(diag[:, i * P:(i + 1) * P], ident[:, 0:P], rs2[:, i:i + 1], None, ALU.mult)
                ins.then_inc(s_diag, 1)
                dve.wait_ge(s_rt, k)

            def h_scale(l, g):
                gains = ga[:, 4 * g:4 * g + 4]
                me.then(V.scalar_tensor_tensor(gains, mod[:, 48 * l + KT + 4 * g:48 * l + KT + 4 * g + 4],
                                               1.0, prm[:, PRM_PRE + KT * l + 4 * g:PRM_PRE + KT * l + 4 * g + 4],
                                               ALU.add, ALU.mult))
                me.wait()
                for t in range(4):
                    k = 4 * g + t
                    V.scalar_tensor_tensor((bufA, bufB)[g % 2][:, t, :], xT[:, k, :], ga[:, k:k + 1], SC[0][:, S:2 * S],
                                           ALU.mult, ALU.mult).then_inc(s_hf, 1)

            def h_low(l, g):
                for t in range(4):
                    k = 4 * g + t
                    dve.wait_ge(s_hhi, KT * l + k + 1)
                    V.scalar_tensor_tensor(H[:, k, S:2 * S], (bufA, bufB)[g % 2][:, t, :], mod[:, 48 * l + k:48 * l + k + 1],
                                           H[:, k, 0:S].bitcast(F32), ALU.add, ALU.subtract).then_inc(s_h, 1)

            V.memset(ones[:, :], 1.0).then_inc(s_tpc, 1)
            me.then(V.memset(cu[:, :, 0:2], 0.0))
            me.then(V.memset(ones_r[:, :].bitcast(F32), 1.0))
            dve.sem_inc(s_used, ADA_START * GROUPS)
            me.then(V.memset(c_cols[:, :, :], 0.0))
            me.wait()
            dve.sem_inc(s_tpc, 1)
            dve.sem_inc(s_z, 4)
            dve.sem_inc(s_yr, 4)
            for i, (col, n) in enumerate(((PRM_B, 96), (PRM_PRE, 112), (PRM_CW, 96))):
                dve.wait_ge(s_tp, i + 1)
                ins = V.tensor_copy(prm[:, col:col + n], Z[i][:, 0:n])
                ins.then_inc(s_tpc, 1)
            dve.wait_ge(s_cs, 2)
            for k in range(ADA_START):
                g, part = k // 2, 1 - k % 2
                dve.wait_ge(s_adapart, GROUPS * (k + 1))
                V.tensor_copy(acc[:, :], row_bank(k)[:, :]).then_inc(s_acc, 1)
                ada_low(k)
                if k == ADA_START - 1:
                    dve.wait_ge(s_mod, k)
                    h_scale(0, g)
                    mods(k, KT * part + 4 * g, 1)
                if ADA_START - LEAD <= k:
                    w = k - (ADA_START - LEAD)
                    split(start_pos(w) % SLOTS, w % 2, ck(0, 0, w))
                if k < ADA_START - 1:
                    mods(k, KT * part + 4 * g, 1)
                if k == 1:
                    dve.wait_ge(s_xsum, KT)
                    rstd(1, SC[0])
                if part == 0:
                    dve.wait_ge(s_mod, k + 1)
                    if k < ADA_START - 1:
                        h_scale(0, g)
                    h_low(0, g)

            for l in range(LAYERS):
                yhi0 = l * (TURNS + GROUPS)
                before = ada_before(l)
                span = CH_TURN + ADA_TURN[l] * GROUPS
                for w in range(LEAD if l == 0 else 2, LEAD):
                    split(stage_pos(l, 0, w) % SLOTS, w % 2, ck(l, 0, w))
                with dve.Fori(0, TURNS) as j:
                    me.loop(j, PER_TURN[l])
                    seen = 0
                    for w in range(LEAD, CH_TURN + LEAD):
                        slot = stage_pos(l, 0, w) % SLOTS
                        if before[w]:
                            rel = stage_pos(l, 0, w) - 1
                            dve.wait_ge(s_stage[rel % SLOTS],
                                        j * (16 * span // SLOTS) + 16 * (rel // SLOTS + 1))
                            ada_chunk(rel % SLOTS, seen % GROUPS, range(ADA_FRONT))
                            low(slot, w % 2, ck(l, j, w))
                            ada_chunk(rel % SLOTS, seen % GROUPS, range(ADA_FRONT, CK))
                            used(ck(l, j, w), 2)
                            seen += 1
                            if seen % GROUPS == 0:
                                dve.sem_inc(s_acc, 1)
                                ada_low(ada_no(l, j, seen // GROUPS - 1))
                        else:
                            split(slot, w % 2, ck(l, j, w))
                        b, late = w // GROUPS - 1, w % GROUPS
                        if late == 0 and b != VV:
                            dst = {QK: bufA, GC: bufB, UU: bufA, GB: bufB, GG: bufA, GR: sg}[b]
                            if b == GB:
                                dve.wait_ge(s_cu, TURNS * l + 1 + j)
                            for t in range(TILES):
                                z_out_of(t, zlo_at(l, j, b) + t + 1, dst[:, t, :])
                        if (b, late) == (VV, 2):
                            for h in range(2):
                                dve.wait_ge(s_sc, 2 * TURNS * l + h + 1 + 2 * j)
                                if h == 0:
                                    dve.wait_ge(s_dec, 16 * (TURNS * l + 1) + 16 * j)
                                V.tensor_tensor(p_sb[:, h, 0:S], SC[h][:, 0:S], dec[:, h, :], ALU.mult)
                                V.tensor_tensor(p_sb[:, h, S:S + P], SC[h][:, S:S + P], dec[:, h, 0:P], ALU.mult)\
                                    .then_inc(s_p, 1)
                        if (b, late) == (GC, 2):
                            for h in range(2):
                                dve.wait_ge(s_in, 2 * TURNS * l + h + 1 + 2 * j)
                                for i in range(NT):
                                    me.then(V.bn_stats(stats[:, 2 * h + i, :], IN[h][:, i * DV:(i + 1) * DV]))
                            me.wait()
                            hold(dve, "dve")
                            for q in range(4):
                                ins = V.bn_aggr(mv[:, q, :], stats[:, q, :])
                            ins.then_inc(s_mv, 1)
                        if (b, late) == (GR, 2):
                            dve.wait_ge(s_yhi, yhi0 + 1 + j)
                            V.tensor_tensor(Y2[:, bass.ds(j * 4, 4), S:2 * S], bufC[:, :, :],
                                            Y2[:, bass.ds(j * 4, 4), 0:S].bitcast(F32), ALU.subtract).then_inc(s_y2, 1)
                        if b == GR and late in (1, 3):
                            if late == 1:
                                dve.wait_ge(s_sgr, TURNS * l + 1 + j)
                                dve.wait_ge(s_tr, 2 * TURNS * l + 2 + 2 * j)
                            for q in (late - 1, late):
                                V.scalar_tensor_tensor(
                                    yr[:, bass.ds(j * 4 + q, 1), :].rearrange("p o s -> p (o s)"),
                                    SC[q // 2][:, (q % 2) * S:(q % 2 + 1) * S],
                                    prm[:, bass.ds(j * 4 + PRM_GN + KT * l + q, 1)], sg[:, q, :],
                                    ALU.mult, ALU.mult).then_inc(s_yr, 1)
                        for k in (k for k in range(CONV_K) if CONV_STEPS[k] == (b, late)):
                            if k == 0:
                                dve.wait_ge(s_cu, TURNS * l + 1 + j)
                                dve.wait_ge(s_tr, 2 * TURNS * l + 2 + 2 * j)
                            for t in range(TILES):
                                wk = prm[:, bass.ds(j * 4 + PRM_CW + 48 * l + KT * k + t, 1)]
                                if k == 0:
                                    ins = V.tensor_scalar(bufC[:, t, :], cu[:, t, 0:S], wk, None, ALU.mult)
                                else:
                                    ins = V.scalar_tensor_tensor(bufC[:, t, :], cu[:, t, k:k + S], wk,
                                                                 bufC[:, t, :], ALU.mult, ALU.add)
                                if k < CONV_K - 1:
                                    me.then(ins)
                            if k < CONV_K - 1:
                                me.wait()
                            else:
                                ins.then_inc(s_cv, 1)
                        if (b, late) == (GG, 2):
                            dve.wait_ge(s_sg, TURNS * l + 1 + j)
                            dve.wait_ge(s_cg, TURNS * l + 1 + j)
                            V.tensor_tensor(bufC[:, :, :], bufC[:, :, :], bufA[:, :, :], ALU.mult).then_inc(s_y, 1)
                        if b in mod_points(l) and late == 1:
                            m = mod_points(l).index(b)
                            al, part = ADA_WHAT[l][m]
                            mods(ada_no(l, j, m), j * 4 + 48 * al + KT * part, b)
                    me.end(TURNS)

                def out_block(nb, first=False, last=False):
                    for w in range(LEAD if first else 1, OUT_CH + (0 if last and l == LAYERS - 1 else 1)):
                        split(w % SLOTS, w % 2, ck_out(l, nb, w))
                        if first and w < LEAD + GROUPS:
                            q = 4 * (w - LEAD)
                            dve.wait_ge(s_yhi, yhi0 + TURNS + w - LEAD + 1)
                            V.tensor_tensor(H[:, q:q + 4, S:2 * S], yr[:, q:q + 4, :],
                                            H[:, q:q + 4, 0:S].bitcast(F32), ALU.subtract).then_inc(s_hr, 1)
                    for t in range(TILES):
                        z_out_of(t, zlo_out(l, nb) + t + 1,
                                 yr[:, bass.ds(nb * 4 + t, 1), :].rearrange("p o s -> p (o s)"))

                dve.wait_ge(s_mod, ada_no(l, TURNS, 0))
                V.tensor_tensor(gp[:, :], mod[:, 48 * l + 2 * KT:48 * l + 3 * KT],
                                prm[:, PRM_POST + KT * l:PRM_POST + KT * l + KT], ALU.mult).then_inc(s_gp, 1)
                dve.wait_ge(s_yr, 4 + 4 * TURNS * (l + 1))
                out_block(0, first=True)
                with dve.Fori(1, 3) as nb:
                    out_block(nb)
                out_block(3, last=True)
                dve.wait_ge(s_osum, l + 1)
                rstd(2 * l + 2, IN[0])
                rstd_o = IN[0][:, S:2 * S].rearrange("p (o s) -> p o s", o=1).broadcast_to([P, 2, S])
                for half in range(2 * POOL_G):
                    tiles = slice(2 * half, 2 * half + 2)
                    dve.wait_ge(s_ou, KT * l + 2 * half + 2)
                    me.then(V.tensor_tensor(yr[:, tiles, :], yr[:, tiles, :], rstd_o, ALU.mult))
                    me.wait()
                    V.tensor_tensor(xT[:, tiles, :], yr[:, tiles, :], xT[:, tiles, :], ALU.add).then_inc(s_xn, 1)
                if l < LAYERS - 1:
                    split(stage_pos(l + 1, 0, 1) % SLOTS, 1, ck(l + 1, 0, 1))
                    dve.wait_ge(s_xsum, KT * (l + 2))
                    rstd(2 * l + 3, SC[0])
                    h_scale(l + 1, 0)
                    for g in range(1, GROUPS):
                        h_scale(l + 1, g)
                        h_low(l + 1, g - 1)
                    h_low(l + 1, GROUPS - 1)
            dve.wait_ge(s_ot, NT * (GROUPS - 1) + 1)
            V.tensor_copy(stage[:, 0, GROUP_ORDER[-1], :], out_bank(GROUPS - 1, 0)[:, :]).then_inc(s_ocv, 1)

        @block.gpsimd
        def _(pool):
            me = Steps(pool, s_pd)
            G = nc.gpsimd

            def step(ins):
                me.then(ins)
                me.wait()

            def rstd(k):
                pool.wait_ge(s_var, k)
                G.tensor_tensor(rs2[:, :], var2[:, :], mhalf[:, 0:NT], ALU.pow).then_inc(s_pow, 1)

            step(G.memset(mhalf[:, :], -0.5))
            ang, u, n = bufC[:, 1, :], bufC[:, 2, :], bufC[:, 3, :]
            pool.wait_ge(s_pos, 16)
            pool.wait_ge(s_par, 16 * 12)
            step(G.tensor_copy(u, bufC[:, 0, :].bitcast(I32)))
            step(G.tensor_scalar(ang, u, ident[:, P:P + 1], None, ALU.mult))
            turn = 2 * math.pi
            c1 = round(turn * 2 ** 9) / 2 ** 9
            c2 = round((turn - c1) * 2 ** 21) / 2 ** 21
            c3 = turn - c1 - c2
            whole = 1.5 * 2 ** 23
            for scale in (2.0 ** 20, 2.0 ** 10, 1.0):
                step(G.tensor_scalar(n, ang, 1.0 / (turn * scale), None, ALU.mult))
                step(G.tensor_scalar(n, n, whole, None, ALU.add))
                step(G.tensor_scalar(n, n, whole, None, ALU.subtract))
                for part in (c1, c2, c3):
                    step(G.tensor_scalar(u, n, part * scale, None, ALU.mult))
                    step(G.tensor_tensor(ang, ang, u, ALU.subtract))
            edge = float(np.nextafter(np.float32(math.pi), np.float32(0)))
            step(G.tensor_scalar(ang, ang, edge, None, ALU.min))
            step(G.tensor_scalar(ang, ang, -edge, None, ALU.max))
            pool.sem_inc(s_tab, 1)
            rstd(1)
            pool.wait_ge(s_sin, 2)
            step(G.tensor_tensor(cos_t[:, :], cos_t[:, :], cos_t[:, :], ALU.mult))
            step(G.tensor_scalar(cos_t[:, :], cos_t[:, :], -2.0, 1.0, ALU.mult, ALU.add))
            step(G.tensor_scalar(sin_t[:, :], sin_t[:, :], ident[:, P + 1:P + 2], None, ALU.mult))

            def all4(t):
                return t[:, :].rearrange("p (o s) -> p o s", o=1).broadcast_to([P, 4, S])

            for l in range(LAYERS):
                with pool.Fori(0, TURNS) as j:
                    me.loop(j, 5)
                    pool.wait_ge(s_z, z_at(l, j, VV))
                    me.then(G.tensor_tensor(bufC[:, :, :], bufA[:, :, :], all4(cos_t), ALU.mult))
                    pool.wait_ge(s_swap, 2 * TURNS * l + 2 + 2 * j)
                    me.then(G.tensor_tensor(bufB[:, :, :], bufB[:, :, :], all4(sin_t), ALU.mult))
                    me.wait()
                    G.tensor_tensor(bufC[:, :, :], bufC[:, :, :], bufB[:, :, :], ALU.add).then_inc(s_rope, 1)
                    pool.wait_ge(s_mv, TURNS * l + 1 + j)
                    hold(pool, "pool")
                    me.then(G.tensor_scalar(rs4[:, :], mv[:, :, 1], EPS, None, ALU.add))
                    me.wait()
                    me.then(G.tensor_tensor(rs4[:, :], rs4[:, :], mhalf[:, :], ALU.pow))
                    me.then(G.tensor_scalar(nb4[:, :], mv[:, :, 0], -1.0, None, ALU.mult))
                    me.wait()
                    G.tensor_tensor(nb4[:, :], nb4[:, :], rs4[:, :], ALU.mult).then_inc(s_rs, 1)
                    pool.wait_ge(s_z, z_at(l, j, GB))
                    G.tensor_tensor(cu[:, :, 2:S + 2], bufA[:, :, :], bufB[:, :, :], ALU.mult).then_inc(s_cu, 1)
                    pool.wait_ge(s_cv, TURNS * l + 1 + j)
                    G.tensor_tensor(bufC[:, :, :], bufC[:, :, :], bufB[:, :, :], ALU.mult).then_inc(s_cg, 1)
                    me.end(TURNS)
                for nb in range(D // BLK - 1):
                    pool.wait_ge(s_o, KT * l + TILES * (nb + 1))
                    if nb == 0:
                        ins = G.tensor_tensor(bufB[:, 0:2, :], bufA[:, 0:2, :], bufA[:, 2:4, :], ALU.add)
                    else:
                        step(G.tensor_tensor(bufB[:, 2:4, :], bufA[:, 0:2, :], bufA[:, 2:4, :], ALU.add))
                        ins = G.tensor_tensor(bufB[:, 0:2, :], bufB[:, 0:2, :], bufB[:, 2:4, :], ALU.add)
                    ins.then_inc(s_opre, 1)
                    pool.wait_ge(s_opre, (D // BLK - 1) * l + nb + 1)
                rstd(2 * l + 2)
                last = slice(4 * POOL_G, 4 * POOL_G + 4)
                pool.wait_ge(s_ou, KT * (l + 1))
                pool.wait_ge(s_rtsb, l + 1)
                step(G.tensor_tensor(yr[:, last, :], yr[:, last, :],
                                     rt_sb.rearrange("p (o s) -> p o s", o=1).broadcast_to([P, 4, S]), ALU.mult))
                G.tensor_tensor(xT[:, last, :], yr[:, last, :], xT[:, last, :], ALU.add).then_inc(s_xp, 1)
                if l < LAYERS - 1:
                    rstd(2 * l + 3)

        @block.tensor
        def _(pe):
            T = nc.tensor
            I = ident[:, 0:P]

            def order(tiles, last):
                if last:
                    return [(t, a) for t in range(tiles) for a in range(CK)]
                return [(t, 2 * h + a) for h in range(2) for t in range(tiles) for a in range(2)]

            def chunk(parity, n, kc, rhs, z, nk=GROUPS, h=None, quarter=None):
                steps = order(TILES, kc == nk - 1)
                if quarter is not None:
                    steps = steps[4 * quarter:4 * quarter + 4]
                for t, a in steps:
                    if kc == 0 and a == 0:
                        pe.wait_ge(s_z, z(t))
                    if t == 0 and a % 2 == 0:
                        pe.wait_ge(s_lo, 2 * n + a // 2 + 1)
                        if h is not None:
                            pe.wait_ge(s_h, h + CK * kc + a + 2)
                    wh = w_hi[:, 2 * parity + a // 2, a % 2, t * P:(t + 1) * P]
                    wl = w_lo[:, 2 * parity + a // 2, a % 2, t * P:(t + 1) * P]
                    act = rhs(CK * kc + a)
                    start = kc == 0 and a == 0
                    stop = kc == nk - 1 and a == CK - 1
                    if start:
                        T.matmul(Z[t][:, :], wh, act, start=True, stop=False)
                    ins = T.matmul(Z[t][:, 0:S], wl, act[:, 0:S], start=False, stop=False)
                    if not start:
                        ins = T.matmul(Z[t][:, :], wh, act, start=False, stop=stop)
                    if kc == nk - 1 and a == CK - 1:
                        ins.then_inc(s_pe, 1)
                    elif kc < nk - 1 and a % 2 and t == TILES - 1:
                        ins.then_inc(s_pe, 2)

            def v_chunk(parity, n, kc, z):
                for i, a in order(NT, kc == GROUPS - 1):
                    if kc == 0 and a == 0:
                        pe.wait_ge(s_z, z(i))
                    if i == 0 and a % 2 == 0:
                        pe.wait_ge(s_lo, 2 * n + a // 2 + 1)
                    wh = w_hi[:, 2 * parity + a // 2, a % 2, :]
                    wl = w_lo[:, 2 * parity + a // 2, a % 2, :]
                    hh = H[:, CK * kc + a, i * P:(i + 1) * P]
                    hl = H[:, CK * kc + a, S + i * P:S + (i + 1) * P]
                    T.matmul(Z[i][:, :], hh, wh, start=kc == 0 and a == 0, stop=False)
                    T.matmul(Z[i][:, :], hh, wl, start=False, stop=False)
                    ins = T.matmul(Z[i][:, :], hl, wh, start=False,
                                   stop=kc == GROUPS - 1 and a == CK - 1)
                    if kc == GROUPS - 1 and a == CK - 1:
                        ins.then_inc(s_pe, 2)
                    elif kc < GROUPS - 1 and a % 2 and i == NT - 1:
                        ins.then_inc(s_pe, 2)

            def ada_sum(k, b):
                pe.wait_ge(s_alo, k + 1)
                for t in range(TILES):
                    dst = ada_bank(b)[:, 2 * t:2 * t + 2]
                    T.matmul(dst, acc_hi[:, t * P:(t + 1) * P], ones_r[:, :], start=True, stop=False)
                    ins = T.matmul(dst, acc_lo[:, t * P:(t + 1) * P], ones_r[:, :], start=False, stop=True)
                ins.then_inc(s_mm, 1)

            def spread(k, banks):
                pe.wait_ge(s_diag, k)
                for bank, done in zip(banks, (s_rt, s_rt2)):
                    T.matmul(bank[:, S:2 * S], ones[:, :], diag, start=True, stop=True).then_inc(done, 1)

            def keep_clock(n):
                for _ in range(n):
                    T.matmul(Z[0][:, 0:P], ones[:, :], ones[:, :], start=True, stop=True)

            def x_sum(k, groups=range(GROUPS)):
                for g in groups:
                    for t in range(4):
                        if t % 2 == 0:
                            pe.wait_ge(s_xsq, 2 * GROUPS * k + 2 * g + t // 2 + 1)
                        T.matmul(SC[0][:, 0:S], ones[:, :], (bufA, bufB)[g % 2][:, t, :], start=g == 0 and t == 0,
                                 stop=g == 3 and t == 3).then_inc(s_xsum, 1)

            pe.wait_ge(s_par, 16 * 12)
            for i, n in enumerate((96, 112, 96)):
                T.transpose(Z[i][:, 0:n], bufA[0:n, i, 0:P], ident[0:n, 0:n]).then_inc(s_tp, 1)

            def x_transposes():
                pe.wait_ge(s_x, 32)
                rows = yr[:, :, :].rearrange("p t s -> p (t s)")
                for g in range(GROUPS):
                    if g >= 2:
                        pe.wait_ge(s_xc, 2 * (g - 1))
                    for i in range(2):
                        for q in range(2):
                            for tok in range(NT):
                                col = tok * D + (4 * g + 2 * i + q) * P
                                ins = T.transpose((SC, IN)[g % 2][i][:, q * S + tok * P:q * S + (tok + 1) * P],
                                                  rows[:, col:col + P], I)
                        ins.then_inc(s_tp, 1)

            def turn(l, j, first=0):
                for b in range(BLOCKS):
                    pb = b - 1 if b else GR
                    z0 = z_at(l, j, b) - (2 if pb == VV else 4)
                    for kc in range(first if b == QK else 0, GROUPS):
                        w = GROUPS * b + kc
                        z = lambda t: z0 + min(t + 1, 2 if pb == VV else 4)
                        if b == VV:
                            v_chunk(w % 2, ck(l, j, w), kc, z)
                        else:
                            chunk(w % 2, ck(l, j, w), kc, lambda k: H[:, k, :], z, h=KT * l if b == QK else None)
                    if b == VV:
                        pe.wait_ge(s_rope, TURNS * l + 1 + j)
                        pe.wait_ge(s_yr, 4 * TURNS * l + 4 + 4 * j)
                        for h in range(2):
                            q, k = bufC[:, h, :], bufC[:, 2 + h, :]
                            T.matmul(SC[h][:, 0:S], k[:, 0:P], q, start=True, stop=True)
                            T.matmul(SC[h][:, S:S + P], k[:, P:S], q[:, P:S], start=True, stop=True).then_inc(s_sc, 1)
                    if b == GC:
                        for h in range(2):
                            pe.wait_ge(s_p, 2 * TURNS * l + h + 1 + 2 * j)
                            pe.wait_ge(s_z, z_at(l, j, GC))
                            v0, v1 = (v_sb[:, i, h * DV:(h + 1) * DV] for i in range(NT))
                            T.matmul(IN[h][:, 0:DV], p_sb[:, h, 0:P], v0, start=True, stop=True)
                            T.matmul(IN[h][:, DV:2 * DV], p_sb[:, h, P:2 * P], v0, start=True, stop=False)
                            T.matmul(IN[h][:, DV:2 * DV], p_sb[:, h, 2 * P:3 * P], v1, start=False, stop=True)\
                                .then_inc(s_in, 1)
                    if b == UU:
                        pe.wait_ge(s_yn, TURNS * l + 1 + j)
                        for h in range(2):
                            for e in range(2):
                                for i in range(NT):
                                    ins = T.transpose(SC[h][:, e * S + i * P:e * S + (i + 1) * P],
                                                      bufC[:, 2 * h + i, e * P:(e + 1) * P], I)
                            ins.then_inc(s_tr, 1)
                    if b in mod_points(l):
                        ada_sum(ada_no(l, j, mod_points(l).index(b)), b)

            pe.sem_inc(s_pe, 8)
            pe.wait_ge(s_tpc, 5)
            pe.wait_ge(s_cs, 2)
            def first_quarters(at):
                for w in range(LEAD - 1):
                    for quarter in range(4):
                        if FIRST_AT[w][quarter] == at:
                            chunk(w % 2, ck(0, 0, w), w, lambda k: H[:, k, :], lambda t: t + 1, h=0, quarter=quarter)

            for k in range(ADA_START):
                if k >= 2:
                    pe.wait_ge(s_acc, k - 1)
                for kc in range(GROUPS):
                    slot, turns_of_ring = start_ada_pos(k, kc) % SLOTS, start_ada_pos(k, kc) // SLOTS
                    pe.wait_ge(s_stage[slot], 16 * (turns_of_ring + 1))
                    for a in range(CK):
                        ins = T.matmul(row_bank(k)[COL * a:COL * (a + 1), :], c_cols[:, CK * kc + a, :],
                                       stage[:, slot, a, :], start=kc == 0, stop=kc == GROUPS - 1)
                    ins.then_inc(s_adapart, 1)
                    if k == 1:
                        x_sum(0, (kc,))
                    if (k, kc) == (3, 0):
                        spread(1, SC[:1])
                    if k > 1 and kc == SUM_AT:
                        pe.wait_ge(s_mod, k - 1)
                        ada_sum(k - 1, GR)
                    first_quarters((k, kc))
                if k == 0:
                    x_transposes()
                if k == 1:
                    ada_sum(0, GR)
            first_quarters((ADA_START, 0))
            pe.wait_ge(s_mod, ADA_START - 1)
            ada_sum(ADA_START - 1, GR)
            first_quarters((ADA_START, 1))

            for l in range(LAYERS):
                if l == 0:
                    turn(0, 0, first=LEAD - 1)
                with nc.Fori(1 if l == 0 else 0, TURNS, engines=(mybir.EngineType.PE,), hint_back_edge=True) as j:
                    turn(l, j)

                def src(k):
                    return Y2[:, k, :] if k < KT else H[:, k - KT, :]

                for nb in range(D // BLK):
                    if nb == 1:
                        pe.wait_ge(s_mod, ada_no(l, TURNS, 0))
                    for w in range(OUT_CH):
                        if nb == 0:
                            if w < GROUPS:
                                pe.wait_ge(s_y2, TURNS * l + w + 1)
                            else:
                                pe.wait_ge(s_hr, GROUPS * l + w - GROUPS + 1)
                        chunk(w % 2, ck_out(l, nb, w), w, src, lambda t: z_out(l, nb) - 4 + t + 1, nk=OUT_CH)
                pe.wait_ge(s_opre, (D // BLK - 1) * (l + 1))
                for t in range(2):
                    T.matmul(IN[0][:, 0:S], ones[:, :], bufB[:, t, :], start=t == 0, stop=False)
                for t in range(TILES):
                    pe.wait_ge(s_o, KT * (l + 1) - TILES + t + 1)
                    ins = T.matmul(IN[0][:, 0:S], ones[:, :], bufA[:, t, :], start=False, stop=t == TILES - 1)
                ins.then_inc(s_osum, 1)
                spread(2 * l + 2, IN)
                if l < LAYERS - 1:
                    keep_clock(CLOCK_X)
                    x_sum(l + 1)
                    keep_clock(CLOCK_SUMS)
                    spread(2 * l + 3, SC[:1])
                    keep_clock(CLOCK_H)
            for n, g in enumerate(GROUP_ORDER):
                if g == POOL_G:
                    pe.wait_ge(s_xp, LAYERS)
                else:
                    pe.wait_ge(s_xn, 2 * (GROUPS + POOL_G * (LAYERS - 1) + g + 1))
                if n == 3:
                    pe.wait_ge(s_oc, NT)
                for i in range(NT):
                    for t in range(4):
                        ins = T.transpose(out_bank(n, i)[:, t * P:(t + 1) * P],
                                          xT[:, 4 * g + t, i * P:(i + 1) * P], I)
                    ins.then_inc(s_ot, 1)


def constants():
    half = DK // 2
    f = (np.float32(10000.0) ** (-np.arange(half, dtype=np.float32) / np.float32(half))).astype(np.float32)
    cst = np.zeros((P, P + 2), np.float32)
    cst[:, :P] = np.eye(P, dtype=np.float32)
    cst[:, P] = np.concatenate([f, f])
    cst[:, P + 1] = np.concatenate([-np.ones(half), np.ones(half)])
    gamma = 1.0 - 2.0 ** (-5.0 - np.arange(HEADS))
    diff = np.arange(S)[None, :] - np.arange(P)[:, None]
    dec = np.where(diff[None] >= 0, gamma[:, None, None] ** np.maximum(diff, 0)[None], 0.0) * DK ** -0.5
    dec = dec.reshape(TURNS, 2, P, S).transpose(0, 2, 1, 3)
    dec = np.concatenate([dec, dec[:1]])
    return cst, np.ascontiguousarray(dec.astype(np.float32))


_INS = ["x", "c", "positions", "norm_pre", "norm_post", "w_ada", "b_ada", "w_in", "conv_w", "gn_gain", "w_out"]


def kernel(**inputs):
    import concourse.bacc as bacc
    from concourse.bass_utils import run_bass_kernel_spmd

    nc = bacc.Bacc("TRN2", target_bir_lowering=False, num_devices=1)
    arrays, args = {}, []
    for name in _INS:
        a = np.ascontiguousarray(inputs[name])
        arrays[f"in_{name}"] = a
        args.append(nc.dram_tensor(f"in_{name}", a.shape, mybir.dt.from_np(a.dtype), kind="ExternalInput").ap())
    for name, a in zip(("consts", "decay"), constants()):
        arrays[name] = a
        args.append(nc.dram_tensor(name, a.shape, F32, kind="ExternalInput").ap())
    args.append(nc.dram_tensor("out", (1, S, D), F32, kind="ExternalOutput").ap())
    build(nc, *args)
    r = run_bass_kernel_spmd(nc, [arrays], core_ids=[0])
    return r.results[0]["out"]
```
